# Optimizing a Trainium2 kernel written in Bass

```python
import math
import jax, jax.numpy as jnp
from jax import lax
import numpy as np
import jax
import jax.numpy as jnp

D_MODEL = 1024
BATCH = 1
SEQ = 512
DEPTH = 2

HEAD_DIM = 64
N_HEADS = 16
D_MIX = N_HEADS * HEAD_DIM
N_HEADS_A = 8
N_KV_A = 2
WINDOW = 128
N_HEADS_B = 4
MOBA_BLOCK = 256
MOBA_TOPK = 3
N_HEADS_C = 4
C_KV_LATENT = 128
N_IDX_HEADS = 4
IDX_DIM = 64
DSA_TOPK = 256
D_FF = 2816
N_BUCKETS = 32
MAX_DISTANCE = 128
RMS_EPS = 1e-6
Q_BLOCK = 128

A_Q = N_HEADS_A * HEAD_DIM
A_KV = N_KV_A * HEAD_DIM
B_QKV = N_HEADS_B * HEAD_DIM
C_Q = N_HEADS_C * HEAD_DIM
C_QIDX = N_IDX_HEADS * IDX_DIM
COL_SIZES = (A_Q, A_KV, A_KV, B_QKV, B_QKV, B_QKV, C_Q, C_KV_LATENT, C_QIDX, IDX_DIM, N_IDX_HEADS)
D_IN = A_Q + 2 * A_KV + 3 * B_QKV + C_Q + C_KV_LATENT + C_QIDX + IDX_DIM + N_IDX_HEADS


def _rmsnorm(x, g):
    x32 = x.astype(jnp.float32)
    y = x32 * lax.rsqrt(jnp.mean(x32 * x32, axis=-1, keepdims=True) + RMS_EPS)
    return (y * g.astype(jnp.float32)).astype(x.dtype)

def _swiglu(x, w_gate, w_up, w_down):
    return (jax.nn.silu(x @ w_gate) * (x @ w_up)) @ w_down

def _t5_bucket(dist):
    n = jnp.maximum(dist, 0)
    max_exact = N_BUCKETS // 2
    nf = jnp.maximum(n, 1).astype(jnp.float32)
    large = max_exact + (jnp.log(nf / max_exact) / math.log(MAX_DISTANCE / max_exact)
                         * (N_BUCKETS - max_exact)).astype(jnp.int32)
    large = jnp.minimum(large, N_BUCKETS - 1)
    return jnp.where(n < max_exact, n, large)

def _split_cols(p):
    cuts = []
    acc = 0
    for sz in COL_SIZES[:-1]:
        acc += sz
        cuts.append(acc)
    return jnp.split(p, cuts, axis=-1)

def _sliding_window_attn(q, k, v, sinks, bias_tab):
    B, T = q.shape[0], q.shape[1]
    nq = T // Q_BLOCK
    G = N_HEADS_A // N_KV_A
    pad = ((0, 0), (WINDOW, 0), (0, 0), (0, 0))
    kp = jnp.pad(k, pad).reshape(B, nq + 1, Q_BLOCK, N_KV_A, HEAD_DIM)
    vp = jnp.pad(v, pad).reshape(B, nq + 1, Q_BLOCK, N_KV_A, HEAD_DIM)
    kb = jnp.concatenate([kp[:, :-1], kp[:, 1:]], axis=2)
    vb = jnp.concatenate([vp[:, :-1], vp[:, 1:]], axis=2)
    qb = q.reshape(B, nq, Q_BLOCK, N_KV_A, G, HEAD_DIM)
    s = jnp.einsum('bnqkgd,bnskd->bnkgqs', qb, kb).astype(jnp.float32) * (HEAD_DIM ** -0.5)
    qi = jnp.arange(Q_BLOCK)[:, None]
    si = jnp.arange(2 * Q_BLOCK)[None, :]
    dist = WINDOW + qi - si
    bias = bias_tab[:, _t5_bucket(dist)].astype(jnp.float32)
    bias = bias.reshape(N_KV_A, G, Q_BLOCK, 2 * Q_BLOCK)
    key_pos = jnp.arange(nq)[:, None] * Q_BLOCK - WINDOW + si
    valid = ((dist >= 0) & (dist < WINDOW))[None] & (key_pos >= 0)[:, None, :]
    s = jnp.where(valid[None, :, None, None], s + bias, -jnp.inf)
    sink = sinks.astype(jnp.float32).reshape(N_KV_A, G)[None, None, :, :, None, None]
    m = jnp.maximum(jnp.max(s, axis=-1, keepdims=True), sink)
    p = jnp.exp(s - m)
    denom = jnp.sum(p, axis=-1, keepdims=True) + jnp.exp(sink - m)
    o = jnp.einsum('bnkgqs,bnskd->bnqkgd', (p / denom).astype(v.dtype), vb)
    return o.reshape(B, T, N_HEADS_A * HEAD_DIM)

def _moba_attn(q, k, v, bias_tab):
    B, T = q.shape[0], q.shape[1]
    nb = -(-T // MOBA_BLOCK)
    Tp = nb * MOBA_BLOCK
    pad = ((0, 0), (0, Tp - T), (0, 0), (0, 0))
    kbh = jnp.pad(k, pad).reshape(B, nb, MOBA_BLOCK, N_HEADS_B, HEAD_DIM).transpose(0, 3, 1, 2, 4)
    vbh = jnp.pad(v, pad).reshape(B, nb, MOBA_BLOCK, N_HEADS_B, HEAD_DIM).transpose(0, 3, 1, 2, 4)
    n_sel = min(MOBA_TOPK, nb - 1)
    scale = HEAD_DIM ** -0.5
    h_idx = jnp.arange(N_HEADS_B)[None, :, None, None]
    b_idx = jnp.arange(B)[:, None, None, None]
    if n_sel > 0:
        k_mean = jnp.mean(kbh.astype(jnp.float32), axis=3)
        gate = jnp.einsum('bthd,bhnd->bhtn', q.astype(jnp.float32), k_mean)
        own_all = jnp.arange(T) // MOBA_BLOCK
        past = jnp.arange(nb)[None, :] < own_all[:, None]
        gate = jnp.where(past[None, None], gate, -jnp.inf)
        _, sel_idx = lax.top_k(gate, n_sel)

    def chunk(i):
        t0 = i * Q_BLOCK
        tq = t0 + jnp.arange(Q_BLOCK)
        qc = lax.dynamic_slice_in_dim(q, t0, Q_BLOCK, axis=1).transpose(0, 2, 1, 3)
        ob = t0 // MOBA_BLOCK
        k_own = lax.dynamic_index_in_dim(kbh, ob, axis=2, keepdims=False)
        v_own = lax.dynamic_index_in_dim(vbh, ob, axis=2, keepdims=False)
        d_own = tq[:, None] - (ob * MOBA_BLOCK + jnp.arange(MOBA_BLOCK))[None, :]
        s_own = (jnp.einsum('bhqd,bhsd->bhqs', qc, k_own).astype(jnp.float32) * scale
                 + bias_tab[:, _t5_bucket(d_own)].astype(jnp.float32)[None])
        s_own = jnp.where((d_own >= 0)[None, None], s_own, -jnp.inf)
        if n_sel == 0:
            p_own = jax.nn.softmax(s_own, axis=-1)
            o = jnp.einsum('bhqs,bhsd->bhqd', p_own.astype(v.dtype), v_own)
            return o.transpose(0, 2, 1, 3)
        idx_c = lax.dynamic_slice_in_dim(sel_idx, t0, Q_BLOCK, axis=2)
        k_sel = kbh[b_idx, h_idx, idx_c]
        v_sel = vbh[b_idx, h_idx, idx_c]
        sel_pos = idx_c[..., None] * MOBA_BLOCK + jnp.arange(MOBA_BLOCK)
        d_sel = tq[None, None, :, None, None] - sel_pos
        b_sel = bias_tab[h_idx[..., None], _t5_bucket(d_sel)].astype(jnp.float32)
        s_sel = jnp.einsum('bhqd,bhqjsd->bhqjs', qc, k_sel).astype(jnp.float32) * scale + b_sel
        ok = (idx_c < (tq // MOBA_BLOCK)[None, None, :, None])[..., None]
        s_sel = jnp.where(ok, s_sel, -jnp.inf).reshape(B, N_HEADS_B, Q_BLOCK, n_sel * MOBA_BLOCK)
        p = jax.nn.softmax(jnp.concatenate([s_sel, s_own], axis=-1), axis=-1).astype(v.dtype)
        p_sel = p[..., :n_sel * MOBA_BLOCK].reshape(B, N_HEADS_B, Q_BLOCK, n_sel, MOBA_BLOCK)
        p_own = p[..., n_sel * MOBA_BLOCK:]
        o = (jnp.einsum('bhqjs,bhqjsd->bhqd', p_sel, v_sel)
             + jnp.einsum('bhqs,bhsd->bhqd', p_own, v_own))
        return o.transpose(0, 2, 1, 3)

    out = lax.map(chunk, jnp.arange(T // Q_BLOCK))
    return out.transpose(1, 0, 2, 3, 4).reshape(B, T, N_HEADS_B * HEAD_DIM)

def _dsa_attn(q, k, v, q_idx, k_idx, w_idx, bias_tab):
    B, T = q.shape[0], q.shape[1]
    n_keep = min(DSA_TOPK, T // 4)
    key_pos = jnp.arange(T)
    b_idx = jnp.arange(B)[:, None, None]
    scale = HEAD_DIM ** -0.5

    def chunk(i):
        t0 = i * Q_BLOCK
        tq = t0 + jnp.arange(Q_BLOCK)
        qi = lax.dynamic_slice_in_dim(q_idx, t0, Q_BLOCK, axis=1)
        wi = lax.dynamic_slice_in_dim(w_idx, t0, Q_BLOCK, axis=1).astype(jnp.float32)
        dots = jnp.einsum('bqhd,bsd->bqhs', qi, k_idx).astype(jnp.float32) * (IDX_DIM ** -0.5)
        score = jnp.einsum('bqhs,bqh->bqs', jax.nn.relu(dots), wi)
        score = jnp.where((key_pos[None, :] <= tq[:, None])[None], score, -jnp.inf)
        _, idx = lax.top_k(score, n_keep)
        k_sel = k[b_idx, idx]
        v_sel = v[b_idx, idx]
        qc = lax.dynamic_slice_in_dim(q, t0, Q_BLOCK, axis=1)
        d = tq[None, :, None] - idx
        bias = bias_tab[:, _t5_bucket(d)].astype(jnp.float32).transpose(1, 0, 2, 3)
        s = jnp.einsum('bqhd,bqkd->bhqk', qc, k_sel).astype(jnp.float32) * scale + bias
        s = jnp.where((d >= 0)[:, None], s, -jnp.inf)
        p = jax.nn.softmax(s, axis=-1).astype(v.dtype)
        return jnp.einsum('bhqk,bqkd->bqhd', p, v_sel)

    out = lax.map(chunk, jnp.arange(T // Q_BLOCK))
    return out.transpose(1, 0, 2, 3, 4).reshape(B, T, N_HEADS_C * HEAD_DIM)

def first_inputs(seed: int = 0) -> dict:
    key = jax.random.key(seed)
    ks = jax.random.split(key, 18)

    def nrm(k, shape, fan_in):
        return jax.random.normal(k, shape, jnp.float32) * (fan_in ** -0.5)

    def gain(k, shape):
        return 1.0 + 0.05 * jax.random.normal(k, shape, jnp.float32)

    return {
        "x": jax.random.normal(ks[0], (BATCH, SEQ, D_MODEL), jnp.float32),
        "rel_bias_table": 0.5 * jax.random.normal(ks[1], (N_BUCKETS, N_HEADS), jnp.float32),
        "ffn1_norm": gain(ks[2], (DEPTH, D_MODEL)),
        "ffn1_w_gate": nrm(ks[3], (DEPTH, D_MODEL, D_FF), D_MODEL),
        "ffn1_w_up": nrm(ks[4], (DEPTH, D_MODEL, D_FF), D_MODEL),
        "ffn1_w_down": nrm(ks[5], (DEPTH, D_FF, D_MODEL), D_FF),
        "mix_norm": gain(ks[6], (DEPTH, D_MODEL)),
        "w_in": nrm(ks[7], (DEPTH, D_MODEL, D_IN), D_MODEL),
        "attn_sinks": 0.5 * jax.random.normal(ks[8], (DEPTH, N_HEADS_A), jnp.float32),
        "kv_norm_c": gain(ks[9], (DEPTH, C_KV_LATENT)),
        "w_kv_up_c": nrm(ks[10], (DEPTH, C_KV_LATENT, 2 * HEAD_DIM), C_KV_LATENT),
        "w_out": nrm(ks[11], (DEPTH, D_MIX, D_MODEL), D_MIX),
        "ffn2_norm": gain(ks[12], (DEPTH, D_MODEL)),
        "ffn2_w_gate": nrm(ks[13], (DEPTH, D_MODEL, D_FF), D_MODEL),
        "ffn2_w_up": nrm(ks[14], (DEPTH, D_MODEL, D_FF), D_MODEL),
        "ffn2_w_down": nrm(ks[15], (DEPTH, D_FF, D_MODEL), D_FF),
        "final_norm": gain(ks[16], (D_MODEL,)),
    }

def first_block(x, rel_bias_table, ffn1_norm, ffn1_w_gate, ffn1_w_up, ffn1_w_down, mix_norm, w_in,
              attn_sinks, kv_norm_c, w_kv_up_c, w_out, ffn2_norm, ffn2_w_gate, ffn2_w_up,
              ffn2_w_down, final_norm):
    B, T = x.shape[0], x.shape[1]
    tab = rel_bias_table.T
    tab_a = tab[:N_HEADS_A]
    tab_b = tab[N_HEADS_A:N_HEADS_A + N_HEADS_B]
    tab_c = tab[N_HEADS_A + N_HEADS_B:]
    for l in range(DEPTH):
        x = x + 0.5 * _swiglu(_rmsnorm(x, ffn1_norm[l]), ffn1_w_gate[l], ffn1_w_up[l], ffn1_w_down[l])
        h = _rmsnorm(x, mix_norm[l])
        (qa, ka, va, qb, kb, vb, qc, ckv, qidx, kidx, widx) = _split_cols(h @ w_in[l])
        out_a = _sliding_window_attn(qa.reshape(B, T, N_HEADS_A, HEAD_DIM),
                                     ka.reshape(B, T, N_KV_A, HEAD_DIM),
                                     va.reshape(B, T, N_KV_A, HEAD_DIM),
                                     attn_sinks[l], tab_a)
        out_b = _moba_attn(qb.reshape(B, T, N_HEADS_B, HEAD_DIM),
                           kb.reshape(B, T, N_HEADS_B, HEAD_DIM),
                           vb.reshape(B, T, N_HEADS_B, HEAD_DIM), tab_b)
        kv_c = _rmsnorm(ckv, kv_norm_c[l]) @ w_kv_up_c[l]
        out_c = _dsa_attn(qc.reshape(B, T, N_HEADS_C, HEAD_DIM),
                          kv_c[..., :HEAD_DIM], kv_c[..., HEAD_DIM:],
                          qidx.reshape(B, T, N_IDX_HEADS, IDX_DIM), kidx,
                          widx * (N_IDX_HEADS ** -0.5), tab_c)
        x = x + jnp.concatenate([out_a, out_b, out_c], axis=-1) @ w_out[l]
        x = x + 0.5 * _swiglu(_rmsnorm(x, ffn2_norm[l]), ffn2_w_gate[l], ffn2_w_up[l], ffn2_w_down[l])
    return _rmsnorm(x, final_norm)


GRID_W = 64
CTX_LEN = 256
A_HEADS = 8
A_KV_HEADS = 2
A_WINDOW = 128
A_BLOCK = 128
B_HEADS = 8
NA_ROWS = 8
NA_COLS = 16
QA_W = A_HEADS * HEAD_DIM
KVA_W = A_KV_HEADS * HEAD_DIM
QKVB_W = B_HEADS * HEAD_DIM
EVEN_SPLITS = (QA_W, QA_W + KVA_W, QA_W + 2 * KVA_W, QA_W + 2 * KVA_W + QKVB_W, QA_W + 2 * KVA_W + 2 * QKVB_W)
EVEN_IN = QA_W + 2 * KVA_W + 3 * QKVB_W
EVEN_OUT = (A_HEADS + B_HEADS) * HEAD_DIM
C_HEADS = 16
C_Q_RANK = 384
C_KV_RANK = 256
C_NOPE = 64
C_ROPE = 32
C_V = 64
C_IN = C_Q_RANK + C_KV_RANK + C_ROPE
C_OUT = C_HEADS * C_V
D_FF_2 = 4 * D_MODEL
N_EVEN = (DEPTH + 1) // 2
N_ODD = DEPTH // 2
ROPE_THETA = 10000.0
NORM_EPS = 1e-6
NEG_INF = -1e30


def rms_norm(x, g):
    xf = x.astype(jnp.float32)
    y = xf * lax.rsqrt(jnp.mean(xf * xf, axis=-1, keepdims=True) + NORM_EPS)
    return (y * g.astype(jnp.float32)).astype(x.dtype)

def modulate(h, shift, scale):
    return h * (1 + scale) + shift

def adaln(cond, w, b):
    m = jax.nn.silu(cond) @ w + b
    return jnp.split(m[:, None, :], 6, axis=-1)

def rope_1d(x, pos):
    half = x.shape[-1] // 2
    inv = ROPE_THETA ** (-jnp.arange(half, dtype=jnp.float32) / half)
    ang = pos.astype(jnp.float32)[:, None] * inv[None, :]
    cos, sin = jnp.cos(ang)[:, None, :], jnp.sin(ang)[:, None, :]
    x1, x2 = x[..., :half], x[..., half:]
    return jnp.concatenate([x1 * cos - x2 * sin, x1 * sin + x2 * cos], axis=-1).astype(x.dtype)

def rope_2d(x, row, col):
    half = x.shape[-1] // 2
    return jnp.concatenate([rope_1d(x[..., :half], row), rope_1d(x[..., half:], col)], axis=-1)

def squared_relu_mlp(h, w1, w2):
    return jnp.square(jax.nn.relu(h @ w1)) @ w2

def ctx_self_attention(q, k, v, scale, sink=None):
    bsz, n, hq, dq = q.shape
    g = k.shape[2]
    r = hq // g
    qg = q.reshape(bsz, n, g, r, dq)
    s = jnp.einsum('bqgrd,bkgd->bgrqk', qg, k, preferred_element_type=jnp.float32) * scale
    if sink is not None:
        sk = jnp.broadcast_to(sink.astype(jnp.float32).reshape(g, r)[None, :, :, None, None], (bsz, g, r, n, 1))
        s = jnp.concatenate([s, sk], axis=-1)
    p = jax.nn.softmax(s, axis=-1)[..., :n].astype(v.dtype)
    o = jnp.einsum('bgrqk,bkgd->bqgrd', p, v)
    return o.reshape(bsz, n, hq * v.shape[-1])

def window_attention(q, k, v, kc, vc, sink):
    bsz, seq, hq, d = q.shape
    g = k.shape[2]
    r = hq // g
    nb = seq // A_BLOCK
    qb = q.reshape(bsz, nb, A_BLOCK, g, r, d)

    def band(t):
        tb = jnp.pad(t.reshape(bsz, nb, A_BLOCK, g, d), ((0, 0), (1, 1), (0, 0), (0, 0), (0, 0)))
        return jnp.concatenate([tb[:, :-2], tb[:, 1:-1], tb[:, 2:]], axis=2)

    kb, vb = band(k), band(v)
    qpos = jnp.arange(seq).reshape(nb, A_BLOCK)
    kpos = (jnp.arange(nb)[:, None] - 1) * A_BLOCK + jnp.arange(3 * A_BLOCK)[None, :]
    valid = ((kpos[:, None, :] >= 0) & (kpos[:, None, :] < seq)
             & (jnp.abs(qpos[:, :, None] - kpos[:, None, :]) <= A_WINDOW))
    scale = d ** -0.5
    s_loc = jnp.einsum('bnqgrd,bnkgd->bngrqk', qb, kb, preferred_element_type=jnp.float32) * scale
    s_loc = jnp.where(valid[None, :, None, None], s_loc, NEG_INF)
    s_ctx = jnp.einsum('bnqgrd,bcgd->bngrqc', qb, kc, preferred_element_type=jnp.float32) * scale
    s_sink = jnp.broadcast_to(sink.astype(jnp.float32).reshape(g, r)[None, None, :, :, None, None],
                              (bsz, nb, g, r, A_BLOCK, 1))
    p = jax.nn.softmax(jnp.concatenate([s_loc, s_ctx, s_sink], axis=-1), axis=-1).astype(v.dtype)
    nloc = 3 * A_BLOCK
    nctx = kc.shape[1]
    o = (jnp.einsum('bngrqk,bnkgd->bnqgrd', p[..., :nloc], vb)
         + jnp.einsum('bngrqc,bcgd->bnqgrd', p[..., nloc:nloc + nctx], vc))
    return o.reshape(bsz, seq, hq * d)

def neighbourhood_attention(q, k, v, kc, vc, rpb, rows_n):
    bsz, _, h, d = q.shape
    kh = min(NA_ROWS, rows_n)
    r = jnp.arange(rows_n)
    row_idx = jnp.clip(r - kh // 2, 0, rows_n - kh)[:, None] + jnp.arange(kh)[None, :]
    cq = jnp.arange(GRID_W)
    c0 = jnp.clip(cq - NA_COLS // 2, 0, GRID_W - NA_COLS)
    col_ok = (cq[None, :] >= c0[:, None]) & (cq[None, :] < c0[:, None] + NA_COLS)
    dri = row_idx - r[:, None] + NA_ROWS - 1
    dci = jnp.clip(cq[None, :] - cq[:, None], 1 - NA_COLS, NA_COLS - 1) + NA_COLS - 1
    bias = rpb.astype(jnp.float32)[:, dri[:, None, :, None], dci[None, :, None, :]]
    bias = jnp.moveaxis(bias, 0, 1)
    qg = q.reshape(bsz, rows_n, GRID_W, h, d)
    kg = k.reshape(bsz, rows_n, GRID_W, h, d)[:, row_idx]
    vg = v.reshape(bsz, rows_n, GRID_W, h, d)[:, row_idx]
    scale = d ** -0.5
    s_loc = jnp.einsum('brqhd,brikhd->brhqik', qg, kg, preferred_element_type=jnp.float32) * scale + bias[None]
    s_loc = jnp.where(col_ok[:, None, :], s_loc, NEG_INF).reshape(bsz, rows_n, h, GRID_W, kh * GRID_W)
    s_ctx = jnp.einsum('brqhd,bchd->brhqc', qg, kc, preferred_element_type=jnp.float32) * scale
    p = jax.nn.softmax(jnp.concatenate([s_loc, s_ctx], axis=-1), axis=-1).astype(v.dtype)
    nloc = kh * GRID_W
    p_loc = p[..., :nloc].reshape(bsz, rows_n, h, GRID_W, kh, GRID_W)
    o = jnp.einsum('brhqik,brikhd->brqhd', p_loc, vg) + jnp.einsum('brhqc,bchd->brqhd', p[..., nloc:], vc)
    return o.reshape(bsz, rows_n * GRID_W, h * d)

def blockwise_dense_attention(q, k, v, kc, vc, scale):
    bsz, seq, h, dq = q.shape
    nb = seq // Q_BLOCK
    kall = jnp.concatenate([kc, k], axis=1)
    vall = jnp.concatenate([vc, v], axis=1)
    qb = jnp.moveaxis(q.reshape(bsz, nb, Q_BLOCK, h, dq), 1, 0)

    def one_block(qblk):
        s = jnp.einsum('bqhd,bkhd->bhqk', qblk, kall, preferred_element_type=jnp.float32) * scale
        p = jax.nn.softmax(s, axis=-1).astype(vall.dtype)
        return jnp.einsum('bhqk,bkhd->bqhd', p, vall)

    o = lax.map(one_block, qb)
    return jnp.moveaxis(o, 0, 1).reshape(bsz, seq, h * v.shape[-1])

def even_mixer(h_lat, h_ctx, row, col, rows_n, w_in, w_out, a_qn, a_kn, a_sink, b_qn, b_kn, b_rpb, need_ctx_out):
    def heads(hh):
        bsz, n, _ = hh.shape
        qa, ka, va, qb, kb, vb = jnp.split(hh @ w_in, EVEN_SPLITS, axis=-1)
        qa = rms_norm(qa.reshape(bsz, n, A_HEADS, HEAD_DIM), a_qn)
        ka = rms_norm(ka.reshape(bsz, n, A_KV_HEADS, HEAD_DIM), a_kn)
        va = va.reshape(bsz, n, A_KV_HEADS, HEAD_DIM)
        qb = rms_norm(qb.reshape(bsz, n, B_HEADS, HEAD_DIM), b_qn)
        kb = rms_norm(kb.reshape(bsz, n, B_HEADS, HEAD_DIM), b_kn)
        vb = vb.reshape(bsz, n, B_HEADS, HEAD_DIM)
        return qa, ka, va, qb, kb, vb

    qa, ka, va, qb, kb, vb = heads(h_lat)
    qa_c, ka_c, va_c, qb_c, kb_c, vb_c = heads(h_ctx)
    qa = rope_2d(qa, row, col)
    ka = rope_2d(ka, row, col)
    o_a = window_attention(qa, ka, va, ka_c, va_c, a_sink)
    o_b = neighbourhood_attention(qb, kb, vb, kb_c, vb_c, b_rpb, rows_n)
    y_lat = jnp.concatenate([o_a, o_b], axis=-1) @ w_out
    y_ctx = None
    if need_ctx_out:
        scale = HEAD_DIM ** -0.5
        oa_c = ctx_self_attention(qa_c, ka_c, va_c, scale, a_sink)
        ob_c = ctx_self_attention(qb_c, kb_c, vb_c, scale)
        y_ctx = jnp.concatenate([oa_c, ob_c], axis=-1) @ w_out
    return y_lat, y_ctx

def mla_project(hh, w_in, qa_norm, kva_norm, w_uq, w_ukv, qn_nope, qn_rope, kn_nope, kn_rope):
    bsz, n, _ = hh.shape
    cq, ckv, kr = jnp.split(hh @ w_in, (C_Q_RANK, C_Q_RANK + C_KV_RANK), axis=-1)
    q = (rms_norm(cq, qa_norm) @ w_uq).reshape(bsz, n, C_HEADS, C_NOPE + C_ROPE)
    kv = (rms_norm(ckv, kva_norm) @ w_ukv).reshape(bsz, n, C_HEADS, C_NOPE + C_V)
    q_nope = rms_norm(q[..., :C_NOPE], qn_nope)
    q_rope = rms_norm(q[..., C_NOPE:], qn_rope)
    k_nope = rms_norm(kv[..., :C_NOPE], kn_nope)
    v = kv[..., C_NOPE:]
    k_rope = rms_norm(kr[:, :, None, :], kn_rope)
    return q_nope, q_rope, k_nope, k_rope, v

def odd_mixer(h_lat, h_ctx, row, col, w_in, qa_norm, kva_norm, w_uq, w_ukv,
              qn_nope, qn_rope, kn_nope, kn_rope, w_out, need_ctx_out):
    q_nope, q_rope, k_nope, k_rope, v = mla_project(h_lat, w_in, qa_norm, kva_norm, w_uq, w_ukv,
                                                    qn_nope, qn_rope, kn_nope, kn_rope)
    q = jnp.concatenate([q_nope, rope_2d(q_rope, row, col)], axis=-1)
    k_rope = rope_2d(k_rope, row, col)
    k = jnp.concatenate([k_nope, jnp.broadcast_to(k_rope, k_nope.shape[:-1] + (C_ROPE,))], axis=-1)
    qc_nope, qc_rope, kc_nope, kc_rope, vc = mla_project(h_ctx, w_in, qa_norm, kva_norm, w_uq, w_ukv,
                                                         qn_nope, qn_rope, kn_nope, kn_rope)
    kc = jnp.concatenate([kc_nope, jnp.broadcast_to(kc_rope, kc_nope.shape[:-1] + (C_ROPE,))], axis=-1)
    scale = (C_NOPE + C_ROPE) ** -0.5
    y_lat = blockwise_dense_attention(q, k, v, kc, vc, scale) @ w_out
    y_ctx = None
    if need_ctx_out:
        qc = jnp.concatenate([qc_nope, qc_rope], axis=-1)
        y_ctx = ctx_self_attention(qc, kc, vc, scale) @ w_out
    return y_lat, y_ctx

def second_inputs(seed: int = 0) -> dict:
    key = jax.random.key(seed)
    ks = jax.random.split(key, 32)
    f32 = jnp.float32

    def nrm(k, shape, fan_in):
        return jax.random.normal(k, shape, f32) * fan_in ** -0.5

    def gain(k, shape):
        return 1.0 + 0.05 * jax.random.normal(k, shape, f32)

    return {
        'x': jax.random.normal(ks[0], (BATCH, SEQ, D_MODEL), f32),
        'c': jax.random.normal(ks[1], (BATCH, D_MODEL), f32),
        'ctx': jax.random.normal(ks[2], (BATCH, CTX_LEN, D_MODEL), f32),
        'c_ctx': jax.random.normal(ks[3], (D_MODEL,), f32),
        'ada_w': nrm(ks[4], (DEPTH, D_MODEL, 6 * D_MODEL), D_MODEL),
        'ada_b': 0.02 * jax.random.normal(ks[5], (DEPTH, 6 * D_MODEL), f32),
        'norm_mix': gain(ks[6], (DEPTH, D_MODEL)),
        'norm_mlp': gain(ks[7], (DEPTH, D_MODEL)),
        'mlp_w1': nrm(ks[8], (DEPTH, D_MODEL, D_FF_2), D_MODEL),
        'mlp_w2': nrm(ks[9], (DEPTH, D_FF_2, D_MODEL), D_FF_2),
        'e_w_in': nrm(ks[10], (N_EVEN, D_MODEL, EVEN_IN), D_MODEL),
        'e_w_out': nrm(ks[11], (N_EVEN, EVEN_OUT, D_MODEL), EVEN_OUT),
        'a_q_norm': gain(ks[12], (N_EVEN, HEAD_DIM)),
        'a_k_norm': gain(ks[13], (N_EVEN, HEAD_DIM)),
        'a_sink': jax.random.normal(ks[14], (N_EVEN, A_HEADS), f32),
        'b_q_norm': gain(ks[15], (N_EVEN, HEAD_DIM)),
        'b_k_norm': gain(ks[16], (N_EVEN, HEAD_DIM)),
        'b_rpb': 0.1 * jax.random.normal(ks[17], (N_EVEN, B_HEADS, 2 * NA_ROWS - 1, 2 * NA_COLS - 1), f32),
        'o_w_in': nrm(ks[18], (N_ODD, D_MODEL, C_IN), D_MODEL),
        'o_qa_norm': gain(ks[19], (N_ODD, C_Q_RANK)),
        'o_kva_norm': gain(ks[20], (N_ODD, C_KV_RANK)),
        'o_w_uq': nrm(ks[21], (N_ODD, C_Q_RANK, C_HEADS * (C_NOPE + C_ROPE)), C_Q_RANK),
        'o_w_ukv': nrm(ks[22], (N_ODD, C_KV_RANK, C_HEADS * (C_NOPE + C_V)), C_KV_RANK),
        'o_qn_nope': gain(ks[23], (N_ODD, C_NOPE)),
        'o_qn_rope': gain(ks[24], (N_ODD, C_ROPE)),
        'o_kn_nope': gain(ks[25], (N_ODD, C_NOPE)),
        'o_kn_rope': gain(ks[26], (N_ODD, C_ROPE)),
        'o_w_out': nrm(ks[27], (N_ODD, C_OUT, D_MODEL), C_OUT),
    }

def second_block(x, c, ctx, c_ctx, ada_w, ada_b, norm_mix, norm_mlp, mlp_w1, mlp_w2,
              e_w_in, e_w_out, a_q_norm, a_k_norm, a_sink, b_q_norm, b_k_norm, b_rpb,
              o_w_in, o_qa_norm, o_kva_norm, o_w_uq, o_w_ukv,
              o_qn_nope, o_qn_rope, o_kn_nope, o_kn_rope, o_w_out):
    seq = x.shape[1]
    rows_n = seq // GRID_W
    t = jnp.arange(seq, dtype=jnp.int32)
    row, col = t // GRID_W, t % GRID_W
    for i in range(DEPTH):
        last = i == DEPTH - 1
        j = i // 2
        sh1, sc1, g1, sh2, sc2, g2 = adaln(c, ada_w[i], ada_b[i])
        csh1, csc1, cg1, csh2, csc2, cg2 = adaln(c_ctx[None, :], ada_w[i], ada_b[i])
        h_lat = modulate(rms_norm(x, norm_mix[i]), sh1, sc1)
        h_ctx = modulate(rms_norm(ctx, norm_mix[i]), csh1, csc1)
        if i % 2 == 0:
            y_lat, y_ctx = even_mixer(h_lat, h_ctx, row, col, rows_n, e_w_in[j], e_w_out[j],
                                      a_q_norm[j], a_k_norm[j], a_sink[j],
                                      b_q_norm[j], b_k_norm[j], b_rpb[j], not last)
        else:
            y_lat, y_ctx = odd_mixer(h_lat, h_ctx, row, col, o_w_in[j], o_qa_norm[j], o_kva_norm[j],
                                     o_w_uq[j], o_w_ukv[j], o_qn_nope[j], o_qn_rope[j],
                                     o_kn_nope[j], o_kn_rope[j], o_w_out[j], not last)
        x = x + g1 * y_lat
        x = x + g2 * squared_relu_mlp(modulate(rms_norm(x, norm_mlp[i]), sh2, sc2), mlp_w1[i], mlp_w2[i])
        if not last:
            ctx = ctx + cg1 * y_ctx
            ctx = ctx + cg2 * squared_relu_mlp(modulate(rms_norm(ctx, norm_mlp[i]), csh2, csc2),
                                               mlp_w1[i], mlp_w2[i])
    return x


def setup_inputs(seed=0):
    out = dict(first_inputs(seed))
    for name, value in second_inputs(seed + 1).items():
        if name != "x":
            out[name + "_2"] = value
    return out


def reference(
    x, rel_bias_table, ffn1_norm, ffn1_w_gate, ffn1_w_up, ffn1_w_down, mix_norm, w_in,
    attn_sinks, kv_norm_c, w_kv_up_c, w_out, ffn2_norm, ffn2_w_gate, ffn2_w_up, ffn2_w_down,
    final_norm, c_2, ctx_2, c_ctx_2, ada_w_2, ada_b_2, norm_mix_2, norm_mlp_2, mlp_w1_2,
    mlp_w2_2, e_w_in_2, e_w_out_2, a_q_norm_2, a_k_norm_2, a_sink_2, b_q_norm_2, b_k_norm_2,
    b_rpb_2, o_w_in_2, o_qa_norm_2, o_kva_norm_2, o_w_uq_2, o_w_ukv_2, o_qn_nope_2, o_qn_rope_2,
    o_kn_nope_2, o_kn_rope_2, o_w_out_2,
):
    x = first_block(
        x, rel_bias_table, ffn1_norm, ffn1_w_gate, ffn1_w_up, ffn1_w_down, mix_norm, w_in,
        attn_sinks, kv_norm_c, w_kv_up_c, w_out, ffn2_norm, ffn2_w_gate, ffn2_w_up, ffn2_w_down,
        final_norm,
    )
    return second_block(
        x, c_2, ctx_2, c_ctx_2, ada_w_2, ada_b_2, norm_mix_2, norm_mlp_2, mlp_w1_2, mlp_w2_2,
        e_w_in_2, e_w_out_2, a_q_norm_2, a_k_norm_2, a_sink_2, b_q_norm_2, b_k_norm_2, b_rpb_2,
        o_w_in_2, o_qa_norm_2, o_kva_norm_2, o_w_uq_2, o_w_ukv_2, o_qn_nope_2, o_qn_rope_2,
        o_kn_nope_2, o_kn_rope_2, o_w_out_2,
    )


_drawn_inputs = setup_inputs


def setup_inputs(seed=0):
    import zlib

    import numpy as np

    out = dict(_drawn_inputs(seed))
    spreads = {}
    factors = {'attn_sinks': 8.0,
     'kv_norm_c': 4.72,
     'norm_mix_2': 6.447,
     'a_q_norm_2': 8.0,
     'a_k_norm_2': 8.0,
     'a_sink_2': 8.0,
     'b_q_norm_2': 8.0,
     'b_k_norm_2': 8.0,
     'b_rpb_2': 8.0,
     'o_qa_norm_2': 8.0,
     'o_kva_norm_2': 6.425,
     'o_qn_nope_2': 8.0,
     'o_qn_rope_2': 8.0,
     'o_kn_nope_2': 8.0,
     'o_kn_rope_2': 8.0}
    for name, (base, spread) in spreads.items():
        noise = np.random.default_rng([zlib.crc32(name.encode()), seed]).standard_normal(out[name].shape)
        drawn = base * np.exp(spread * noise) if base else spread * noise
        out[name] = jnp.asarray(drawn.astype(out[name].dtype))
    for name, factor in factors.items():
        out[name] = (out[name] * factor).astype(out[name].dtype)
    return out
```

```python
from contextlib import ExitStack

import numpy as np
import concourse.bass as bass
from concourse import mybir

F32 = mybir.dt.float32
F32R = mybir.dt.float32r
ACT = mybir.ActivationFunctionType
ALU = mybir.AluOpType
AX = mybir.AxisListType.X

D = 1024
KC = D // 128
T = 512
CT = 256
NQ = T // 128
HD = 64
DEPTH = 2
FF1 = 2816
FF2 = 4096
EPS = 1e-6
BIG = 1e30
NO_MAX = 3e38

CH1 = FF1 // 256
CH2 = FF2 // 256
W_IN_COLS = 2244
N_IN1 = -(-W_IN_COLS // 128)
LAYER1_TILES = 2 * CH1 * 6 + N_IN1 + 8
EVEN_COLS = 2304
N_INE = EVEN_COLS // 128
EVEN_TILES = N_INE + 8
MLP_TILES = CH2 * 4
ODD_PAIRS = 8
ODD_TILES = 6 + 2 * ODD_PAIRS + 8
TOPK_ROUNDS = 128 // 8


def program(nc, io):
    top = ExitStack()
    uid = [0]

    def name(base):
        uid[0] += 1
        return f"{base}_{uid[0]}"

    def sb(ctx, base, shape, dt=F32):
        return ctx.enter_context(nc.sbuf_tensor(name(base), shape, dt))

    with top:
        ps = top.enter_context(nc.psum_tensor("ps", [128, 8, 512], F32))
        X = sb(top, "x", [128, KC, T])
        ident = sb(top, "ident", [128, 128])
        ones = sb(top, "ones", [128, 128])
        head_ones = sb(top, "head_ones", [128, 128])
        eps = sb(top, "eps", [128, 1])
        vecs = sb(top, "vecs", [128, io["vecs"].shape[1]])
        mod = sb(top, "mod", [128, DEPTH, 48, 2])
        mod_x = sb(top, "mod_x", [128, DEPTH, 2, KC, 2])
        near_read, near_stored, near_staged = ([top.enter_context(nc.semaphore(name(base))) for _ in range(2)]
                                               for base in ("near_read", "near_stored", "near_staged"))
        ada_landed = [top.enter_context(nc.semaphore(name("ada_landed"))) for _ in range(2)]
        cond_in, mask_in = (top.enter_context(nc.semaphore(name(base))) for base in ("cond_in", "mask_in"))
        silu_cond = nc.dram_tensor("silu_cond", [2, D], F32, kind="Internal").ap()
        bias_line = nc.dram_tensor("bias_line", [16, 640], F32, kind="Internal").ap()
        bias_rows = nc.dram_tensor("bias_rows", [16, 128, 640], F32, kind="Internal").ap()
        near_bias = nc.dram_tensor("near_bias", [8, 128, 896], F32, kind="Internal").ap()

        class Sems:

            def __init__(self):
                self.ctx = ExitStack()
                self.all = []

            def __call__(self, base):
                s = self.ctx.enter_context(nc.semaphore(name(base)))
                self.all.append(s)
                return s

            def clear(self):
                nums = sorted(s.num for s in self.all)
                at = 0
                while at < len(nums):
                    end = at
                    while end + 1 < len(nums) and nums[end + 1] == nums[end] + 1:
                        end += 1
                    nc.sync.sem_clear(range(nums[at], nums[end] + 1))
                    at = end + 1
                nc.all_engine_barrier()

            def close(self):
                self.clear()
                self.ctx.close()

        def vec(key, n=KC, at=0):
            a = io["vec_at"][key] + at
            return vecs[:, a:a + n]

        class Stream:

            def __init__(self, ctx, S, tiles, n_raw, n_hl, total=None):
                self.tiles, self.n_raw, self.n_hl = tiles, n_raw, n_hl
                self.total = total or tiles.shape[0]
                self.raw = sb(ctx, "w_raw", [128, n_raw, 1024])
                self.hi = sb(ctx, "w_hi", [128, n_hl, 1024], F32R)
                self.lo = sb(ctx, "w_lo", [128, n_hl, 1024], F32R)
                self.landed = [S("w_landed") for _ in range(n_raw)]
                self.hi_done, self.lo_done, self.used = S("w_hi_done"), S("w_lo_done"), S("w_used")

            def load(self, sp, base=0):
                R = self.n_raw
                rounds, rest = divmod(self.total, R)

                def fetch(r, n):
                    at = base + n
                    src = self.tiles[at] if isinstance(at, int) else \
                        self.tiles[bass.ds(at, 1)].rearrange("a p n -> (a p) n")
                    sp.dma_start(self.raw[:, r, :], src).then_inc(self.landed[r], 16)

                for r in range(R):
                    fetch(r, r)
                with sp.Fori(1, rounds) as i:
                    for r in range(R):
                        sp.wait_ge(self.lo_done, i * R + (r + 1 - R))
                        fetch(r, i * R + r)
                for r in range(rest):
                    n = rounds * R + r
                    sp.wait_ge(self.lo_done, n - R + 1)
                    fetch(r, n)

            def split_hi(self, act, n, i=0, step=0):
                if n >= self.total:
                    return
                R, H = self.n_raw, self.n_hl
                act.wait_ge(self.landed[n % R], 16 * (n // R + 1) + i * (16 * step // R))
                if n >= H:
                    act.wait_ge(self.used, n - H + 1 + i * step)
                act.activation(self.hi[:, n % H, :], self.raw[:, n % R, :], ACT.Copy).then_inc(self.hi_done, 1)

            def split_lo(self, dve, n, i=0, step=0):
                if n >= self.total:
                    return
                dve.wait_ge(self.hi_done, n + 1 + i * step)
                dve.tensor_tensor(self.lo[:, n % self.n_hl, :], self.raw[:, n % self.n_raw, :],
                                  self.hi[:, n % self.n_hl, :].bitcast(F32), ALU.subtract
                                  ).then_inc(self.lo_done, 1)

            def start(self, split, eng):
                for n in range(self.n_hl):
                    split(eng, n)

            def ready(self, pe, n, i=0, step=0):
                pe.wait_ge(self.lo_done, n + 1 + i * step)

            def pair_at(self, a, b):
                assert self.n_hl == 2
                return self.hi[:, :, a:b], self.lo[:, :, a:b]

            def at(self, n, a, b):
                s = n % self.n_hl
                return self.hi[:, s, a:b], self.lo[:, s, a:b]

        def mm3(pe, out, lhs, rhs, start, stop):
            pe.matmul(out, lhs[0], rhs[0], start=start, stop=False)
            pe.matmul(out, lhs[0], rhs[1], start=False, stop=False)
            return pe.matmul(out, lhs[1], rhs[0], start=False, stop=stop)

        class Norm:

            def __init__(self, S, tmp, src, n, gain, shift, out, bank=7, nk=KC):
                self.src, self.n, self.gain, self.shift, self.out, self.bank = src, n, gain, shift, out, bank
                self.nk, self.tmp = nk, tmp
                self.sq_done, self.sum_done, self.root_done, self.inv_done = S("sq"), S("sum"), S("root"), S("inv")
                self.scaled, self.hi_done, self.lo_done = S("scaled"), S("norm_hi"), S("norm_lo")

            def acc(self):
                return ps[:, self.bank, 0:self.n]

            def scalar(self, act, src_ready=None):
                sq, root, h = self.tmp["sq"], self.tmp["root"], self.tmp["h"]
                for c in range(self.nk):
                    if src_ready:
                        src_ready(act, c)
                    if c >= 2:
                        act.wait_ge(self.sum_done, c - 1)
                    act.activation(sq[:, c % 2, 0:self.n], self.src(c), ACT.Square).then_inc(self.sq_done, 1)
                act.wait_ge(self.sum_done, self.nk)
                act.activation(root[:, 0:self.n], self.acc(), ACT.Ln, bias=eps[:, 0:1],
                               scale=1.0 / (128 * self.nk)).then_inc(self.root_done, 1)
                act.wait_ge(self.root_done, 1)
                act.activation(self.tmp["inv"][:, 0:self.n], root[:, 0:self.n], ACT.Exp, scale=-0.5
                               ).then_inc(self.inv_done, 1)
                for c in range(self.nk):
                    act.wait_ge(self.scaled, c + 1)
                    if self.shift is None:
                        m = act.activation(self.out(0, c), h[:, c % 3, 0:self.n], ACT.Copy)
                    else:
                        m = act.activation(self.out(0, c), h[:, c % 3, 0:self.n], ACT.Identity,
                                           bias=self.shift(c))
                    m.then_inc(self.hi_done, 1)

            def tensor(self, pe):
                for c in range(self.nk):
                    pe.wait_ge(self.sq_done, c + 1)
                    pe.matmul(self.acc(), ones[:, :], self.tmp["sq"][:, c % 2, 0:self.n], start=(c == 0),
                              stop=(c == self.nk - 1)).then_inc(self.sum_done, 1)

            def vector(self, dve):
                inv, h = self.tmp["inv"], self.tmp["h"]

                def scale(c):
                    dve.scalar_tensor_tensor(out=h[:, c % 3, 0:self.n], in0=self.src(c), scalar=self.gain(c),
                                             in1=inv[:, 0:self.n], op0=ALU.mult, op1=ALU.mult
                                             ).then_inc(self.scaled, 1)

                def rest(c):
                    dve.wait_ge(self.hi_done, c + 1)
                    hi = self.out(0, c).bitcast(F32)
                    if self.shift is None:
                        m = dve.tensor_tensor(self.out(1, c), h[:, c % 3, 0:self.n], hi, ALU.subtract)
                    else:
                        m = dve.scalar_tensor_tensor(out=self.out(1, c), in0=h[:, c % 3, 0:self.n],
                                                     scalar=self.shift(c), in1=hi, op0=ALU.add, op1=ALU.subtract)
                    m.then_inc(self.lo_done, 1)

                dve.wait_ge(self.inv_done, 1)
                scale(0)
                for c in range(1, self.nk):
                    if c >= 3:
                        dve.wait_ge(self.lo_done, c - 2)
                    scale(c)
                    rest(c - 1)
                rest(self.nk - 1)
                dve.wait_ge(self.lo_done, self.nk)

        class Mlp:

            def __init__(self, ctx, S, st, first, streams, swiglu, gains, buffers=None):
                self.st, self.n0, self.streams, self.swiglu, self.gains = st, first, streams, swiglu, gains
                self.up = 4 if swiglu else 2
                self.per = self.up + 2
                self.chunks = CH1 if swiglu else CH2
                if buffers:
                    self.mid, self.val, self.hi, self.lo = buffers.mid, buffers.val, buffers.hi, buffers.lo
                else:
                    self.mid = [sb(ctx, "mid", [128, 2, s["n"]]) for s in streams]
                    self.val = [sb(ctx, "val", [128, 2, s["n"]]) for s in streams]
                    self.hi = [sb(ctx, "a_hi", [128, 4, s["n"]], F32R) for s in streams]
                    self.lo = [sb(ctx, "a_lo", [128, 4, s["n"]], F32R) for s in streams]
                self.mid_done, self.val_done = S("mid"), S("val")
                self.hi_done, self.lo_done = S("a_hi"), S("a_lo")
                self.down_done, self.x_done = S("down"), S("x_done")

            def up_tile(self, c, k):
                return self.n0 + (k if c == 0 else self.up + (c - 1) * self.per + k)

            def down_tile(self, c, g):
                if c == self.chunks - 1:
                    return self.n0 + self.up + c * self.per + g
                return self.n0 + self.up + c * self.per + self.up + g

            def up_bank(self, j, s):
                return 2 * j + s

            def run(self, eng, up, down):
                up(0, 0, 0)
                body = self.chunks - 1
                unroll = 2
                for c in range(1, 1 + unroll):
                    up(c, 0, 0)
                    down(c - 1, 0, 0)
                left = (body - unroll - 1) // unroll
                with eng.Fori(1, 1 + left) as i:
                    for c in range(1, 1 + unroll):
                        up(c, i, unroll)
                        down(c - 1, i, unroll)
                for c in range(1 + unroll * (1 + left), self.chunks):
                    up(c, 0, 0)
                    down(c - 1, 0, 0)
                down(self.chunks - 1, 0, 0)

            def tensor(self, pe, h_ready):
                st = self.st

                def up(c, i, u):
                    step = u * self.per
                    for k in range(self.up):
                        n = self.up_tile(c, k)
                        j = k // 2 if self.swiglu else k
                        st.ready(pe, n, i, step)
                        if c >= 1 and (k % 2 == 0 or not self.swiglu):
                            pe.wait_ge(self.val_done, self.vals(c - 1, j) + i * (u * 2))
                        for s, stream in enumerate(self.streams):
                            bank = self.up_bank(j, k % 2 if self.swiglu else s)
                            for kk in range(KC):
                                if c == 0 and k == 0:
                                    h_ready(pe, s, kk)
                                hh, hl = stream["h"]
                                m = mm3(pe, ps[:, bank, 0:stream["n"]], st.at(n, kk * 128, kk * 128 + 128),
                                        (hh[:, kk, :], hl[:, kk, :]), kk == 0, kk == KC - 1)
                        m.then_inc(st.used, 1)

                def down(c, i, u):
                    step = u * self.per
                    pe.wait_ge(self.lo_done, 2 * c + 2 + i * (2 * u))
                    for g in range(2):
                        n = self.down_tile(c, g)
                        st.ready(pe, n, i, step)
                        for q in range(4):
                            o = 8 * c + 4 * g + q
                            lag = 4 if len(self.streams) == 1 else 2
                            if o >= lag or not isinstance(i, int):
                                pe.wait_ge(self.x_done, o - lag + 1 + i * (8 * u))
                            for s, stream in enumerate(self.streams):
                                for f in range(2):
                                    a = 2 * (c % 2) + f
                                    m = mm3(pe, ps[:, self.down_bank(o, s), 0:stream["n"]],
                                            st.at(n, f * 512 + q * 128, f * 512 + q * 128 + 128),
                                            (self.hi[s][:, a, :], self.lo[s][:, a, :]), f == 0, f == 1)
                            m.then_inc(self.down_done if q < 3 else st.used, 1)

                self.run(pe, up, down)

            def vals(self, c, j):
                return 2 * c + j + 1

            def down_bank(self, o, s):
                return 4 + o % 4 if len(self.streams) == 1 else 4 + 2 * (o % 2) + s

            def scalar(self, act):
                st = self.st

                def up(c, i, u):
                    step = u * self.per
                    for k in range(self.up):
                        n = self.up_tile(c, k)
                        st.split_hi(act, n + st.n_hl, i, step)
                        if self.swiglu and k % 2 == 0:
                            continue
                        j = k // 2 if self.swiglu else k
                        act.wait_ge(st.used, n + 1 + i * step)
                        if c >= 1:
                            act.wait_ge(self.val_done, self.vals(c - 1, j) + i * (2 * u))
                        for s, stream in enumerate(self.streams):
                            bank = self.up_bank(j, 0 if self.swiglu else s)
                            m = act.activation(self.mid[s][:, j, :], ps[:, bank, 0:stream["n"]],
                                               ACT.Silu if self.swiglu else ACT.Relu)
                        m.then_inc(self.mid_done, 1)
                        act.wait_ge(self.val_done, self.vals(c, j) + i * (2 * u))
                        for s, stream in enumerate(self.streams):
                            m = act.activation(self.hi[s][:, 2 * (c % 2) + j, :], self.val[s][:, j, :], ACT.Copy)
                        m.then_inc(self.hi_done, 1)

                def down(c, i, u):
                    for g in range(2):
                        st.split_hi(act, self.down_tile(c, g) + st.n_hl, i, u * self.per)

                self.run(act, up, down)

            def vector(self, dve):
                st = self.st

                def rest(c, j, i, u):
                    dve.wait_ge(self.hi_done, self.vals(c, j) + i * (2 * u))
                    for s, stream in enumerate(self.streams):
                        a = 2 * (c % 2) + j
                        m = dve.tensor_tensor(self.lo[s][:, a, :], self.val[s][:, j, :],
                                              self.hi[s][:, a, :].bitcast(F32), ALU.subtract)
                    m.then_inc(self.lo_done, 1)

                def up(c, i, u):
                    step = u * self.per
                    for k in range(self.up):
                        n = self.up_tile(c, k)
                        st.split_lo(dve, n + st.n_hl, i, step)
                        if self.swiglu and k % 2 == 0:
                            continue
                        j = k // 2 if self.swiglu else k
                        dve.wait_ge(self.mid_done, self.vals(c, j) + i * (2 * u))
                        if c >= 1:
                            dve.wait_ge(self.lo_done, self.vals(c - 1, j) + i * (2 * u))
                        for s, stream in enumerate(self.streams):
                            other = ps[:, self.up_bank(j, 1), 0:stream["n"]] if self.swiglu else self.mid[s][:, j, :]
                            m = dve.tensor_tensor(self.val[s][:, j, :], self.mid[s][:, j, :], other, ALU.mult)
                        m.then_inc(self.val_done, 1)
                        if c == 0 or j == 0:
                            rest(c, j, i, u)

                def down(c, i, u):
                    step = u * self.per
                    for g in range(2):
                        n = self.down_tile(c, g)
                        for q in range(4):
                            if q < 3:
                                dve.wait_ge(self.down_done, 3 * (2 * c + g) + q + 1 + i * (6 * u))
                            else:
                                dve.wait_ge(st.used, n + 1 + i * step)
                            o = 4 * g + q
                            for s, stream in enumerate(self.streams):
                                m = dve.scalar_tensor_tensor(
                                    out=stream["x"][:, o, :], in0=ps[:, self.down_bank(8 * c + o, s), 0:stream["n"]],
                                    scalar=self.gains(s, o), in1=stream["x"][:, o, :], op0=ALU.mult, op1=ALU.add)
                            m.then_inc(self.x_done, 1)
                            if g == 0 and q == 1 and c < self.chunks - 1:
                                rest(c + 1, 1, i, u)
                        st.split_lo(dve, n + st.n_hl, i, step)

                self.run(dve, up, down)

            def x_ready(self, eng, c):
                eng.wait_ge(self.x_done, 8 * self.chunks - 8 + c + 1)

        class Project:

            def __init__(self, S, st, first, streams, gains):
                self.st, self.n0, self.streams, self.gains = st, first, streams, gains
                self.x_done = S("proj_x")

            def tensor(self, pe, o_ready):
                o_ready(pe)
                for g in range(2):
                    for p in range(4):
                        n = self.n0 + 4 * g + p
                        self.st.ready(pe, n)
                        if g == 1 and p == 0 and len(self.streams) > 1:
                            pe.wait_ge(self.x_done, 4)
                        for s, stream in enumerate(self.streams):
                            for q in range(4):
                                for f in range(2):
                                    m = mm3(pe, ps[:, self.bank(g, q, s), 0:stream["n"]],
                                            self.st.at(n, f * 512 + q * 128, f * 512 + q * 128 + 128),
                                            (stream["h"][0][:, 2 * p + f, :], stream["h"][1][:, 2 * p + f, :]),
                                            p == 0 and f == 0, p == 3 and f == 1)
                        m.then_inc(self.st.used, 1)

            def bank(self, g, q, s):
                return q + 4 * (g if len(self.streams) == 1 else s)

            def scalar(self, act):
                for n in range(8):
                    self.st.split_hi(act, self.n0 + n + self.st.n_hl)

            def vector(self, dve):
                for n in range(8):
                    self.st.split_lo(dve, self.n0 + n + self.st.n_hl)
                    if n % 4 == 3:
                        dve.wait_ge(self.st.used, self.n0 + n + 1)
                        for q in range(4):
                            o = n // 4 * 4 + q
                            for s, stream in enumerate(self.streams):
                                gain = self.gains(s, o)
                                acc = ps[:, self.bank(n // 4, q, s), 0:stream["n"]]
                                x = stream["x"][:, o, :]
                                if gain is None:
                                    m = dve.tensor_tensor(x, acc, x, ALU.add)
                                else:
                                    m = dve.scalar_tensor_tensor(out=x, in0=acc, scalar=gain, in1=x,
                                                                 op0=ALU.mult, op1=ALU.add)
                            m.then_inc(self.x_done, 1)

            def x_ready(self, eng, c):
                eng.wait_ge(self.x_done, c + 1)

        class Attention:

            def __init__(self, S, tmp, units, groups, turns, q_wide=None):
                self.units, self.groups, self.turns, self.tmp, self.q_wide = units, groups, turns, tmp, q_wide
                self.q_zero, self.q_ready = S("q_zero"), S("q_ready")
                self.scored, self.biased, self.piece_done, self.exped = S("scored"), S("biased"), S("piece"), S("exped")
                self.turned, self.by_act, self.by_dve, self.pv_done = S("turned"), S("pt_act"), S("pt_dve"), S("pv")
                self.arg_done, self.sink_done, self.den_done, self.inv_done = S("arg"), S("sink"), S("den"), S("inv")
                self.out_done = S("o_norm")
                self.chunk_turned, self.chunk_hi, self.chunk_lo = S("ot"), S("ot_hi"), S("ot_lo")
                self.tgroups = []
                self.t_end = []
                self.act_n, self.dve_n = [0], [0]
                for u, unit in enumerate(units):
                    nb = len(unit["v"])
                    for b in range(0, nb, 4):
                        self.tgroups.append((u, b, min(4, nb - b)))
                    self.t_end.append(len(self.tgroups))
                self.pieces = []
                n = 0
                for unit in units:
                    self.pieces.append(n)
                    n += len(unit["keys"]) - 1
                self.sinks_before = [sum(g["minus_sinks"] is not None for g in groups[:k]) for k in range(len(groups) + 1)]
                self.turn_at, self.turn_n = {}, {}
                n = 0
                for g in sorted(turns):
                    self.turn_at[min(8 * g + 8, len(units) - 1)] = g
                    self.turn_n[g] = n
                    n += len(turns[g]) // 4
                self.turn_total = n

            def range_of(self, u):
                return range(self.t_end[u - 1] if u else 0, self.t_end[u])

            @staticmethod
            def evacs(t, odd):
                return (t + 1 - odd) // 2

            def scores_ps(self, u, a, b):
                return ps[:, 2 * (u % 2):2 * (u % 2) + 2, :].rearrange("p a n -> p (a n)")[:, a:b]

            def tensor(self, pe, ready):
                tmp, units = self.tmp, self.units
                turns_done = [0]
                ready(pe)

                def score(u):
                    if u >= len(units):
                        return
                    q = units[u]["q"]
                    if self.q_wide is not None:
                        pe.wait_ge(self.q_ready, u + 1)
                        q = self.q_wide[:, u % 4, :]
                    if u >= 2:
                        pe.wait_ge(self.biased, u - 1)
                    for k, col, n, _ in units[u]["keys"]:
                        m = pe.matmul(self.scores_ps(u, col, col + n), q, k, start=True, stop=True)
                    m.then_inc(self.scored, 1)

                def turn(g):
                    pe.wait_ge(self.out_done, g + 1)
                    for c in range(0, len(self.turns[g]), 4):
                        if turns_done[0] >= 2:
                            pe.wait_ge(self.chunk_lo, turns_done[0] - 1)
                        for j in range(4):
                            m = pe.transpose(ps[:, 4 + turns_done[0] % 2, 128 * j:128 * j + 128],
                                             self.turns[g][c + j][0], ident[:, :])
                        m.then_inc(self.chunk_turned, 1)
                        turns_done[0] += 1

                def turn_probabilities(u):
                    pe.wait_ge(self.exped, u + 1)
                    for t in self.range_of(u):
                        _, b, nb = self.tgroups[t]
                        if t >= 2:
                            pe.wait_ge(self.by_dve if t % 2 else self.by_act, self.evacs(t - 1, t % 2))
                        if turns_done[0]:
                            pe.wait_ge(self.chunk_lo, turns_done[0])
                        for j in range(nb):
                            m = pe.transpose(ps[:, 4 + t % 2, 128 * j:128 * j + 128],
                                             tmp["s"][:, u % 2, 128 * (b + j):128 * (b + j) + 128], ident[:, :])
                        m.then_inc(self.turned, 1)

                def copied(u):
                    for odd, s in ((0, self.by_act), (1, self.by_dve)):
                        if self.evacs(self.t_end[u], odd):
                            pe.wait_ge(s, self.evacs(self.t_end[u], odd))

                def values(u):
                    copied(u)
                    g = u // 8
                    if u % 8 == 0 and g >= 2:
                        pe.wait_ge(self.out_done, g - 1)
                    for b, v in enumerate(units[u]["v"]):
                        m = pe.matmul(ps[:, 6 + g % 2, 64 * (u % 8):64 * (u % 8) + 64],
                                      tmp["pt"][:, u % 2, 128 * b:128 * b + 128], v,
                                      start=(b == 0), stop=(b == len(units[u]["v"]) - 1))
                    m.then_inc(self.pv_done, 1)

                score(0)
                score(1)
                for u in range(len(units) + 1):
                    if u < len(units):
                        turn_probabilities(u)
                        score(u + 2)
                    if u >= 1:
                        values(u - 1)
                    if u - 1 in self.turn_at:
                        copied(min(u, len(units) - 1))
                        turn(self.turn_at[u - 1])

            def copy_pt(self, eng, copy, t, sem):
                u, b, nb = self.tgroups[t]
                eng.wait_ge(self.turned, t + 1)
                if u >= 2:
                    eng.wait_ge(self.pv_done, u - 1)
                copy(self.tmp["pt"][:, u % 2, 128 * b:128 * (b + nb)], ps[:, 4 + t % 2, 0:128 * nb]).then_inc(sem, 1)

            def scalar(self, act, ready=None):
                tmp, units = self.tmp, self.units

                def exp(u):
                    if u >= len(units):
                        return
                    n = 128 * len(units[u]["v"])
                    act.wait_ge(self.biased, u + 1)
                    if u % 8 == 0 and u >= 16:
                        act.wait_ge(self.out_done, u // 8 - 1)
                    act.activation(tmp["s"][:, u % 2, 0:n], tmp["s"][:, u % 2, 0:n], ACT.Exp,
                                   bias=tmp["nm"][:, u % 16:u % 16 + 1], scale=-1.0,
                                   accum_out=tmp["sums"][:, u % 16:u % 16 + 1]).then_inc(self.exped, 1)
                    g = u // 8
                    if u % 8 == 7 and self.groups[g]["minus_sinks"] is not None:
                        act.wait_ge(self.arg_done, self.sinks_before[g] + 1)
                        act.activation(tmp["es"][:, :], tmp["arg"][:, :], ACT.Exp).then_inc(self.sink_done, 1)

                def widen(u):
                    if self.q_wide is None or u >= len(units):
                        return
                    if u >= 4:
                        act.wait_ge(self.scored, u - 3)
                    r = slice(64 * (u % 2), 64 * (u % 2) + 64)
                    act.activation(self.q_wide[r, u % 4, :], units[u]["q"], ACT.Copy).then_inc(self.q_ready, 1)

                if self.q_wide is not None:
                    ready(act)
                    act.wait_ge(self.q_zero, 1)
                for u in range(4):
                    widen(u)
                exp(0)
                exp(1)
                for u in range(len(units) + 1):
                    for t in self.range_of(u) if u < len(units) else ():
                        if t % 2 == 0:
                            self.copy_pt(act, lambda o, i: act.activation(o, i, ACT.Copy), t, self.by_act)
                    exp(u + 2)
                    widen(u + 4)
                    if u - 1 in self.turn_at:
                        g = self.turn_at[u - 1]
                        for c in range(0, len(self.turns[g]), 4):
                            k = self.turn_n[g] + c // 4
                            act.wait_ge(self.chunk_turned, k + 1)
                            for j in range(4):
                                m = act.activation(self.turns[g][c + j][1], ps[:, 4 + k % 2, 128 * j:128 * j + 128],
                                                   ACT.Copy)
                            m.then_inc(self.chunk_hi, 1)

            def vector(self, dve, before_unit=None, ready=None):
                tmp, units = self.tmp, self.units

                def bias(u):
                    if u >= len(units):
                        return
                    unit = units[u]
                    if before_unit:
                        before_unit(dve, u)
                    dve.wait_ge(self.scored, u + 1)
                    if u >= 2:
                        dve.wait_ge(self.turned, self.t_end[u - 2])
                    if u % 8 == 0 and u >= 16:
                        dve.wait_ge(self.out_done, u // 8 - 1)
                    at, nm, last = 0, tmp["nm"][:, u % 16:u % 16 + 1], len(unit["keys"]) - 1
                    for k, (_, col, n, b) in enumerate(unit["keys"]):
                        if k:
                            dve.wait_ge(self.piece_done, self.pieces[u] + k)
                        m = dve.tensor_tensor_reduce(
                            tmp["s"][:, u % 2, at:at + n], self.scores_ps(u, col, col + n), b, 1.0,
                            unit["init"] if k == 0 else tmp["part"][:, (u + k + 1) % 2:(u + k + 1) % 2 + 1],
                            ALU.add, ALU.min, nm if k == last else tmp["part"][:, (u + k) % 2:(u + k) % 2 + 1])
                        m.then_inc(self.biased if k == last else self.piece_done, 1)
                        at += n
                    g = u // 8
                    if u % 8 == 7 and self.groups[g]["minus_sinks"] is not None:
                        dve.wait_ge(self.biased, u + 1)
                        if self.sinks_before[g]:
                            dve.wait_ge(self.sink_done, self.sinks_before[g])
                        r = 8 * (g % 2)
                        dve.tensor_tensor(tmp["arg"][:, :], tmp["nm"][:, r:r + 8], self.groups[g]["minus_sinks"],
                                          ALU.subtract).then_inc(self.arg_done, 1)

                def normalise(g):
                    r = 8 * (g % 2)
                    sums, inv = tmp["sums"][:, r:r + 8], tmp["inv"][:, r:r + 8]
                    dve.wait_ge(self.exped, 8 * g + 8)
                    if self.groups[g]["minus_sinks"] is not None:
                        dve.wait_ge(self.sink_done, self.sinks_before[g] + 1)
                        dve.tensor_tensor(tmp["den"][:, :], sums, tmp["es"][:, :], ALU.add).then_inc(self.den_done, 1)
                        dve.wait_ge(self.den_done, self.sinks_before[g] + 1)
                        sums = tmp["den"][:, :]
                    dve.reciprocal(inv, sums).then_inc(self.inv_done, 1)
                    dve.wait_ge(self.inv_done, g + 1)
                    dve.wait_ge(self.pv_done, 8 * g + 8)
                    if self.groups[g]["free_after"] is not None:
                        dve.wait_ge(self.chunk_turned, self.groups[g]["free_after"])
                    out, shape = self.groups[g]["out"], self.groups[g]["shape"]
                    acc = ps[:, 6 + g % 2, :].rearrange("p (a b d) -> p a b d", a=shape[0], b=shape[1])
                    dve.tensor_tensor(out, acc, inv.rearrange("p (a b d) -> p a b d", a=shape[0], d=1)
                                      .broadcast_to([128, shape[0], shape[1], 64]), ALU.mult
                                      ).then_inc(self.out_done, 1)

                if self.q_wide is not None:
                    if ready:
                        ready(dve)
                    dve.memset(self.q_wide[:, :, :], 0.0).then_inc(self.q_zero, 1)
                bias(0)
                bias(1)
                for u in range(len(units) + 1):
                    for t in self.range_of(u) if u < len(units) else ():
                        if t % 2:
                            self.copy_pt(dve, lambda o, i: dve.tensor_copy(o, i), t, self.by_dve)
                    bias(u + 2)
                    if u >= 1 and (u - 1) % 8 == 7:
                        normalise((u - 1) // 8)
                    if u - 1 in self.turn_at:
                        g = self.turn_at[u - 1]
                        for c in range(0, len(self.turns[g]), 4):
                            k = self.turn_n[g] + c // 4
                            dve.wait_ge(self.chunk_hi, k + 1)
                            for j in range(4):
                                hi, lo = self.turns[g][c + j][1:]
                                m = dve.tensor_tensor(lo, ps[:, 4 + k % 2, 128 * j:128 * j + 128],
                                                      hi.bitcast(F32), ALU.subtract)
                            m.then_inc(self.chunk_lo, 1)

            def all_turned(self, pe):
                pe.wait_ge(self.chunk_lo, self.turn_total)

        def attention_temps(ctx, scores, pt):
            return {"s": scores, "pt": pt,
                    "nm": sb(ctx, "nm", [128, 16]), "sums": sb(ctx, "sums", [128, 16]),
                    "inv": sb(ctx, "inv8", [128, 16]), "den": sb(ctx, "den", [128, 8]),
                    "arg": sb(ctx, "arg", [128, 8]), "es": sb(ctx, "es", [128, 8]), "part": sb(ctx, "part", [128, 2])}


        class HeadTiles:

            def __init__(self, S, work, st, items, rot=None, cos=None, sin=None):
                self.items, self.st, self.w, self.rot, self.cos, self.sin = items, st, work, rot, cos, sin
                self.projected, self.sq_done, self.raw_done, self.sum_done = S("proj"), S("hsq"), S("raw"), S("hsum")
                self.root_done, self.inv_done, self.t_done = S("hroot"), S("hinv"), S("ht")
                self.rotated, self.cos_done, self.sin_done, self.out_done = S("rot"), S("cos"), S("sin"), S("hout")
                self.norms = [sum(not x["plain"] for x in items[:k]) for k in range(len(items) + 1)]
                self.parts = [sum(not x["tiles"] for x in items[:k]) for k in range(len(items) + 1)]
                self.ropes = [sum(x["rope"] for x in items[:k]) for k in range(len(items) + 1)]

            def bank(self, i, a, b):
                return ps[:, 2 * (i % 2):2 * (i % 2) + 2, :].rearrange("p a n -> p (a n)")[:, a:b]

            @staticmethod
            def halves(n):
                return [(0, min(n, 512))] + ([(512, n)] if n > 512 else [])

            def tensor(self, pe):
                items, w = self.items, self.w
                for i in range(len(items) + 2):
                    if i < len(items):
                        if i >= 2:
                            pe.wait_ge(self.raw_done, i - 1)
                        items[i]["project"](pe, i, self.st.used if items[i]["tiles"] else self.projected)
                    if 1 <= i <= len(items) and not items[i - 1]["plain"]:
                        k, it = i - 1, items[i - 1]
                        pe.wait_ge(self.sq_done, self.norms[k] + 1)
                        if self.norms[k]:
                            pe.wait_ge(self.root_done, self.norms[k])
                        for a, b in self.halves(it["n"]):
                            m = pe.matmul(ps[:, 4 + a // 512, 0:b - a], it["ones"], w["sq"][:, self.norms[k] % 2, a:b],
                                          start=True, stop=True)
                        m.then_inc(self.sum_done, 1)
                    if 2 <= i and items[i - 2]["rope"]:
                        k = i - 2
                        pe.wait_ge(self.t_done, self.norms[k] + 1)
                        if self.ropes[k]:
                            pe.wait_ge(self.sin_done, self.ropes[k])
                        pe.matmul(ps[:, 6, 0:512], self.rot, w["t"][:, self.norms[k] % 2, 0:512], start=True, stop=True
                                  ).then_inc(self.rotated, 1)

            def scalar(self, act):
                items, w = self.items, self.w
                for i in range(len(items) + 1):
                    if i < len(items):
                        it = items[i]
                        for n in it["tiles"]:
                            self.st.split_hi(act, n + self.st.n_hl)
                        if it["tiles"]:
                            act.wait_ge(self.st.used, it["tiles"][-1] + 1)
                        else:
                            act.wait_ge(self.projected, self.parts[i] + 1)
                        if it["plain"]:
                            for dst, src, scale in it["copies"](i):
                                m = act.activation(dst, src, ACT.Copy, scale=scale)
                        else:
                            if self.norms[i] >= 2:
                                act.wait_ge(self.sum_done, self.norms[i] - 1)
                            act.activation(w["sq"][:, self.norms[i] % 2, 0:it["n"]], self.bank(i, 0, it["n"]), ACT.Square
                                           ).then_inc(self.sq_done, 1)
                            if self.norms[i] >= 2:
                                act.wait_ge(self.t_done, self.norms[i] - 1)
                            m = act.activation(w["raw"][:, self.norms[i] % 2, 0:it["n"]], self.bank(i, 0, it["n"]), ACT.Copy)
                        m.then_inc(self.raw_done, 1)
                    if i >= 1 and not items[i - 1]["plain"]:
                        k, it = i - 1, items[i - 1]
                        act.wait_ge(self.sum_done, self.norms[k] + 1)
                        if self.norms[k]:
                            act.wait_ge(self.inv_done, self.norms[k])
                        act.activation(w["root"][:, 0:it["n"]],
                                       ps[:, 4:6, :].rearrange("p a n -> p (a n)")[:, 0:it["n"]], ACT.Ln,
                                       bias=eps[:, 0:1], scale=it["scale"]).then_inc(self.root_done, 1)
                        act.wait_ge(self.root_done, self.norms[k] + 1)
                        if self.norms[k]:
                            act.wait_ge(self.t_done, self.norms[k])
                        act.activation(w["inv"][:, 0:it["n"]], w["root"][:, 0:it["n"]], ACT.Exp, scale=-0.5
                                       ).then_inc(self.inv_done, 1)

            def vector(self, dve):
                items, w = self.items, self.w
                for i in range(len(items) + 2):
                    if i < len(items):
                        for n in items[i]["tiles"]:
                            self.st.split_lo(dve, n + self.st.n_hl)
                    if 1 <= i <= len(items) and not items[i - 1]["plain"]:
                        k, it = i - 1, items[i - 1]
                        n = it["n"]
                        dve.wait_ge(self.inv_done, self.norms[k] + 1)
                        dve.wait_ge(self.raw_done, k + 1)
                        if it["rope"]:
                            if k >= 1 and self.ropes[k - 1]:
                                dve.wait_ge(self.out_done, self.ropes[k - 1])
                            dve.scalar_tensor_tensor(out=w["t"][:, self.norms[k] % 2, 0:n], in0=w["raw"][:, self.norms[k] % 2, 0:n],
                                                     scalar=it["gain"], in1=w["inv"][:, 0:n], op0=ALU.mult,
                                                     op1=ALU.mult).then_inc(self.t_done, 1)
                        else:
                            for r, dst in it["dst"]:
                                m = dve.scalar_tensor_tensor(out=dst(0, n), in0=w["raw"][r, self.norms[k] % 2, 0:n],
                                                             scalar=it["gain"][r, :], in1=w["inv"][r, 0:n],
                                                             op0=ALU.mult, op1=ALU.mult)
                            m.then_inc(self.t_done, 1)
                    if 2 <= i and items[i - 2]["rope"]:
                        k, it = i - 2, items[i - 2]
                        t = w["t"][:, self.norms[k] % 2, :]
                        if self.ropes[k]:
                            dve.wait_ge(self.out_done, self.ropes[k])
                        dve.wait_ge(self.t_done, self.norms[k] + 1)
                        dve.tensor_tensor(w["cos"][:, :], t[:, 0:512], self.cos, ALU.mult).then_inc(self.cos_done, 1)
                        dve.wait_ge(self.rotated, self.ropes[k] + 1)
                        dve.tensor_tensor(w["sin"][:, :], ps[:, 6, 0:512], self.sin, ALU.mult
                                          ).then_inc(self.sin_done, 1)
                        dve.wait_ge(self.cos_done, self.ropes[k] + 1)
                        dve.wait_ge(self.sin_done, self.ropes[k] + 1)
                        for r, dst in it["dst"]:
                            m = dve.tensor_tensor(dst(0, 512), w["cos"][r, :], w["sin"][r, :], ALU.add)
                            if it["n"] > 512:
                                m = dve.tensor_copy(dst(512, it["n"]), w["t"][r, self.norms[k] % 2, 512:it["n"]])
                        m.then_inc(self.out_done, 1)

            def all_out(self, eng):
                eng.wait_ge(self.raw_done, len(self.items))
                if self.norms[-1]:
                    eng.wait_ge(self.t_done, self.norms[-1])
                if self.ropes[-1]:
                    eng.wait_ge(self.out_done, self.ropes[-1])

        def setup():
            S = Sems()
            with ExitStack() as ctx:
                tab = sb(ctx, "bias_table", [33, 16])
                hot = sb(ctx, "bucket_lines", [33, 2, 640])
                line = sb(ctx, "line", [8, 2, 640])
                cond = sb(ctx, "cond", [2, D])
                cond_done = S("cond_done")
                loaded, small, line_done, line_out = S("loaded"), S("small"), S("line_done"), S("line_out")
                line_mm, const = S("line_mm"), S("const")
                with nc.Block(no_gpsimd_drain=True) as block:
                    @block.sync
                    def _(sp):
                        for dst, src in ((ident, "ident"), (ones, "ones"), (head_ones, "head_ones"), (vecs, "vecs"),
                                         (tab, "bias_table"), (hot, "bucket_lines"), (cond, "cond")):
                            sp.dma_start(dst[:], io[src]).then_inc(small, 16)
                        sp.dma_start(X[:], io["x"]).then_inc(loaded, 16)
                        sp.wait_ge(line_done, 4)
                        sp.dma_start(bias_line.rearrange("(a h) n -> h a n", a=2), line[:]).then_inc(line_out, 16)
                        sp.wait_ge(line_out, 16)
                        sp.dma_start(bias_rows, bass.AP(bias_line.tensor, 0, [[640, 16], [0, 128], [1, 640]])
                                     ).then_inc(line_out, 16)
                        sp.wait_ge(cond_done, 1)
                        sp.dma_start(silu_cond, cond[:]).then_inc(line_out, 16)
                        sp.wait_ge(line_out, 48)
                        sp.wait_ge(loaded, 16)

                    @block.scalar
                    def _(act):
                        act.wait_ge(small, 112)
                        act.activation(cond[:], cond[:], ACT.Silu).then_inc(cond_done, 1)

                    @block.tensor
                    def _(pe):
                        pe.wait_ge(small, 112)
                        for a in range(2):
                            for b, n in ((0, 512), (1, 128)):
                                m = pe.matmul(ps[0:8, 2 * a + b, 0:n], tab[:, 8 * a:8 * a + 8],
                                              hot[:, a, 512 * b:512 * b + n], start=True, stop=True)
                        m.then_inc(line_mm, 1)

                    @block.vector
                    def _(dve):
                        dve.memset(eps[:], EPS).then_inc(const, 1)
                        dve.wait_ge(line_mm, 1)
                        for a in range(2):
                            for b, n in ((0, 512), (1, 128)):
                                dve.tensor_copy(line[:, a, 512 * b:512 * b + n], ps[0:8, 2 * a + b, 0:n]
                                                ).then_inc(line_done, 1)
                S.close()

        def conditioning(CX):
            S = Sems()
            with ExitStack() as ctx:
                ctx_in, summed = S("ctx_in"), S("summed")
                sq, root, inv = sb(ctx, "sq", [128, 2, T]), sb(ctx, "root", [128, T]), sb(ctx, "inv", [128, T])
                sq_done, sum_done, root_done, inv_done = S("sq"), S("sum"), S("root"), S("inv")

                with nc.Block(no_gpsimd_drain=True) as block:
                    @block.sync
                    def _(sp):
                        sp.dma_start(CX[:], io["ctx"]).then_inc(ctx_in, 16)
                        sp.wait_ge(ctx_in, 16)

                    @block.scalar
                    def _(act):
                        for c in range(KC):
                            if c >= 2:
                                act.wait_ge(sum_done, c - 1)
                            act.activation(sq[:, c % 2, :], X[:, c, :], ACT.Square).then_inc(sq_done, 1)
                        act.wait_ge(sum_done, KC)
                        act.activation(root[:, :], ps[:, 5, :], ACT.Ln, bias=eps[:, 0:1], scale=1.0 / D
                                       ).then_inc(root_done, 1)
                        act.wait_ge(root_done, 1)
                        act.activation(inv[:, :], root[:, :], ACT.Exp, scale=-0.5).then_inc(inv_done, 1)

                    @block.tensor
                    def _(pe):
                        for c in range(KC):
                            pe.wait_ge(sq_done, c + 1)
                            pe.matmul(ps[:, 5, :], ones[:, :], sq[:, c % 2, :], start=(c == 0), stop=(c == KC - 1)
                                      ).then_inc(sum_done, 1)

                    @block.vector
                    def _(dve):
                        for layer in range(DEPTH):
                            b = vec(f"ada_b{layer}", 48).rearrange("p (k s) -> p k s", s=1).broadcast_to([128, 48, 2])
                            dve.tensor_tensor(mod[:, layer], mod[:, layer], b, ALU.add).then_inc(summed, 1)
                        dve.wait_ge(summed, DEPTH)
                        for layer in range(DEPTH):
                            for half, key, at in ((0, "norm_mix", 8), (1, "norm_mlp", 32)):
                                gain = vec(f"{key}{layer}").rearrange("p (k s) -> p k s", s=1).broadcast_to([128, KC, 2])
                                dve.scalar_tensor_tensor(out=mod_x[:, layer, half], in0=mod[:, layer, at:at + 8, :],
                                                         scalar=1.0, in1=gain, op0=ALU.add, op1=ALU.mult
                                                         ).then_inc(summed, 1)
                        dve.wait_ge(inv_done, 1)
                        for c in range(KC):
                            dve.scalar_tensor_tensor(out=X[:, c, :], in0=X[:, c, :], scalar=vec("final_norm", 1, c),
                                                     in1=inv[:, :], op0=ALU.mult, op1=ALU.mult)
                S.close()

        def first_block():
            with ExitStack() as ctx:
                Hh, Hl = sb(ctx, "h_hi", [128, KC, T], F32R), sb(ctx, "h_lo", [128, KC, T], F32R)
                near = sb(ctx, "bias_a", [128, 8, 256])
                far = sb(ctx, "bias_bc", [128, 8, 512])
                lv = sb(ctx, "layer_vecs", [128, 33])
                upc = sb(ctx, "w_kv_up", [128, 192])
                nsink = sb(ctx, "minus_sinks", [128, 8])
                tri = sb(ctx, "causal", [128, 128])
                shared = sb(ctx, "shared", [128, 15, T])
                QA, QB, QC = shared[:, 0:4, :], shared[:, 4:6, :], shared[:, 6:8, :]
                KB, VB = shared[:, 8:10, :], shared[:, 10:12, :].rearrange("p a n -> p (a n)").rearrange(
                    "p (q n) -> p q n", n=256)
                KD, VA = shared[:, 12:14, :], shared[:, 14, :].rearrange("p (q n) -> p q n", n=128)
                CKV, KCc = sb(ctx, "ckv", [128, T]), sb(ctx, "kc", [128, T])
                VC, QI, KI = sb(ctx, "vc", [128, NQ, 64]), sb(ctx, "q_idx", [128, 2, T]), sb(ctx, "k_idx", [128, T])
                WI = sb(ctx, "w_idx", [128, NQ, 4])
                work = sb(ctx, "topk", [128, 1152])
                best = sb(ctx, "best8", [128, 8])
                scratch = sb(ctx, "scratch", [128, 8, 512])
                first_layers(ctx, shared, Hh, Hl, near, far, lv, upc, nsink, tri, QA, KD, VA, QB, KB, VB, QC, CKV, KCc, VC,
                             QI, KI, WI, work, best, scratch)

        def first_layers(ctx, shared, Hh, Hl, near, far, lv, upc, nsink, tri, QA, KD, VA, QB, KB, VB, QC, CKV, KCc, VC,
                         QI, KI, WI, work, best, scratch):
            S = Sems()
            q_wide = sb(ctx, "q_wide", [128, 4, 128])
            flat = shared[:, :, :].rearrange("p a n -> p (a n)")
            ada_w, ada_prod, cond = (flat[:, a:a + 2048].rearrange("p (s n) -> p s n", s=2) for a in (0, 2048, 4096))
            ada_part = flat[:, 6144:7680]
            mod_flat = mod[:, :, :, :].rearrange("p l k s -> p (l k s)")
            near_step = S("near_step")
            ada_step, ada_done = S("ada_step"), S("ada_done")
            relu, comb, O = scratch[:, 0:2, :], scratch[:, 6:8, :], scratch[:, 4:6, :]
            st = Stream(ctx, S, io["w_first"], 3, 3, LAYER1_TILES)
            nt = {"sq": scratch[:, 0:2, :], "root": scratch[:, 2, :], "inv": scratch[:, 3, :], "h": scratch[:, 4:7, :]}
            at = attention_temps(ctx, scratch[:, 0:2, :], scratch[:, 2:4, :])
            stream = {"n": T, "h": (Hh, Hl), "x": X}
            small, vecs_in = S("small"), S("vecs_in")

            def out(part, c):
                return (Hh, Hl)[part][:, c, :]

            norms = [Norm(S, nt, lambda c: X[:, c, :], T, (lambda c, k=k: lv[:, 8 * k + c:8 * k + c + 1]), None, out,
                          bank=0) for k in range(3)]
            n_mix, n_out, n_f2 = 6 * CH1, 6 * CH1 + N_IN1, 6 * CH1 + N_IN1 + 8
            mlp_a = Mlp(ctx, S, st, 0, [stream], True, lambda s, o: 0.5)
            mlp_b = Mlp(ctx, S, st, n_f2, [stream], True, lambda s, o: 0.5, mlp_a)
            proj = Project(S, st, n_out, [stream], lambda s, o: None)

            order = [("T", [(QI[:, 0, :], 0, 128, 1.0)]), ("T", [(QI[:, 1, :], 0, 128, 1.0)]),
                     ("KI", [(KI[0:64, :], 0, 64, 1.0), (KI[64:128, :], 0, 64, 1.0)]),
                     ("T", [(CKV[:, :], 0, 128, 1.0)]),
                     ("T", [(KD[64 * d:64 * d + 64, g, :], 64 * g, 64 * g + 64, 1.0)
                            for g in range(2) for d in range(2)]),
                     ("V", VA[:, :, :])]
            order += [("T", [(QA[:, c, :], 0, 128, -0.125)]) for c in range(4)]
            order += [("T", [(QB[:, c, :], 0, 128, -0.125)]) for c in range(2)]
            order += [("T", [(KB[:, c, :], 0, 128, 1.0)]) for c in range(2)]
            order += [("V", VB[:, :, 128 * c:128 * c + 128]) for c in range(2)]
            order += [("T", [(QC[:, c, :], 0, 128, -0.125)]) for c in range(2)]
            assert len(order) == N_IN1
            IDX_AFTER, CKV_AFTER = 4, 7
            evac, idx_mm, relu_done, acc_done = S("evac"), S("idx_mm"), S("relu"), S("acc")
            ckv_sq, ckv_sum, ckv_root, ckv_inv, ckv_n = S("ckv_sq"), S("ckv_sum"), S("ckv_root"), S("ckv_inv"), S("ckv_n")
            kv_mm, kv_out, topk, sel_done, comb_done = S("kv_mm"), S("kv_out"), S("topk"), S("sel"), S("comb")
            nsink_done = S("nsink")
            spans = {1: (0, 256), 2: (256, 640), 3: (640, 1152)}

            units, comb_of = [], {}
            for qb in range(NQ):
                qs = slice(128 * qb, 128 * qb + 128)
                nk = 128 * (qb + 1)
                for h in range(16):
                    r = slice(64 * (h % 2), 64 * (h % 2) + 64)
                    if h < 8:
                        k0 = max(0, qb - 1) * 128
                        units.append({"q": QA[r, h // 2, qs], "init": nsink[:, h:h + 1],
                                      "keys": [(KD[:, h // 4, k0:nk], 0, nk - k0, near[:, h, 256 - (nk - k0):256])],
                                      "v": [VA[:, j, 64 * (h // 4):64 * (h // 4) + 64] for j in range(k0 // 128, qb + 1)]})
                    elif h < 12:
                        units.append({"q": QB[r, (h - 8) // 2, qs], "init": NO_MAX,
                                      "keys": [(KB[:, (h - 8) // 2, 0:nk], 0, nk, far[:, h - 8, 512 - nk:512])],
                                      "v": [VB[:, j, 64 * (h - 8):64 * (h - 8) + 64] for j in range(qb + 1)]})
                    else:
                        bias = far[:, h - 8, 512 - nk:512]
                        if qb:
                            comb_of[len(units)] = len(comb_of)
                            bias = comb[:, comb_of[len(units)] % 2, 0:nk]
                        units.append({"q": QC[r, (h - 12) // 2, qs], "init": NO_MAX,
                                      "keys": [(KCc[:, 0:nk], 0, nk, bias)],
                                      "v": [VC[:, j, :] for j in range(qb + 1)]})
            groups = [{"out": O[:, g % 2, :].rearrange("p (a b d) -> p a b d", a=1, d=64), "shape": (1, 8),
                       "minus_sinks": nsink[:, :] if g % 2 == 0 else None,
                       "free_after": 2 * (g // 2) if g >= 2 else None} for g in range(2 * NQ)]
            turns = {2 * qb + 1: [(O[:, c // 4, 128 * (c % 4):128 * (c % 4) + 128],
                                   Hh[:, c, 128 * qb:128 * qb + 128], Hl[:, c, 128 * qb:128 * qb + 128])
                                  for c in range(8)] for qb in range(NQ)}
            att = Attention(S, at, units, groups, turns, q_wide)

            def topk_rounds():
                state = {"n": 0, "sem": 3}

                def one(dve):
                    n = state["n"]
                    if n >= 3 * TOPK_ROUNDS:
                        return False
                    qb, r = n // TOPK_ROUNDS + 1, n % TOPK_ROUNDS
                    a, e = spans[qb]
                    dve.wait_ge(topk, state["sem"])
                    dve.max(best[:, :], work[:, a:e]).then_inc(topk, 1)
                    dve.wait_ge(topk, state["sem"] + 1)
                    dve.match_replace(work[:, a:e], best[:, :], work[:, a:e], -3e38).then_inc(topk, 1)
                    state["sem"] += 2
                    if r == TOPK_ROUNDS - 1:
                        dve.wait_ge(topk, state["sem"])
                        dve.tensor_scalar(work[:, a:e], work[:, a:e], -2e38, BIG, ALU.is_gt, ALU.mult
                                          ).then_inc(sel_done, 1)
                    state["n"] += 1
                    return True

                return one

            with nc.Fori(0, DEPTH) as layer:
                with nc.Block() as block:
                    @block.sync
                    def _(sp):
                        sp.dma_start(lv[:], io["layer_vecs"][bass.ds(layer, 1)].rearrange("a p n -> (a p) n")
                                     ).then_inc(vecs_in, 16)
                        st.load(sp, layer * LAYER1_TILES)

                    @block.gpsimd
                    def _(pool):
                        def conditioning_half(half):
                            first = 24 * half

                            def fetch(n, i=0):
                                pool.dma_start(ada_w[:, n % 2, :],
                                               io["w_ada"][bass.ds(layer * 48 + first + n + i * 4, 1)]
                                               .rearrange("a p n -> (a p) n")).then_inc(ada_landed[n % 2], 16)

                            def step(i, k, more=True):
                                n = first + k
                                before = 1 + 6 * n + i * 24
                                if k == 0:
                                    for stored in near_stored:
                                        pool.wait_ge(stored, layer * 32 + 32)
                                    pool.wait_ge(cond_in, layer * 32 + 16 * (half + 1))
                                pool.wait_ge(ada_landed[k % 2], layer * 384 + 16 * (n // 2 + 1) + i * 32)
                                pool.wait_ge(ada_step, before)
                                w = ada_w[:, k % 2:k % 2 + 1, :].broadcast_to([128, 2, 1024])
                                pool.tensor_tensor(ada_prod, w, cond, ALU.mult).then_inc(ada_step, 1)
                                for level, m in enumerate((512, 256, 128, 64, 32)):
                                    pool.wait_ge(ada_step, before + 1 + level)
                                    if level == 0 and more:
                                        fetch(k + 2, i)
                                    out = ada_prod[:, :, 0:m] if m > 32 else \
                                        ada_part[:, bass.ds(64 * k + i * 256, 64)].rearrange("p (s n) -> p s n", s=2)
                                    pool.tensor_tensor(out, ada_prod[:, :, 0:m], ada_prod[:, :, m:2 * m], ALU.add
                                                       ).then_inc(ada_step, 1)

                            pool.dma_start(flat[:, 4096:6144], bass.AP(silu_cond.tensor, 0, [[0, 128], [1, 2048]])
                                           ).then_inc(cond_in, 16)
                            fetch(0)
                            fetch(1)
                            with pool.Fori(0, 5) as i:
                                for k in range(4):
                                    step(i, k)
                            for k in range(20, 24):
                                step(0, k, k + 2 < 24)

                        def neighbourhood_biases():
                            raw, out = (flat[:, a:a + 1792].rearrange("p (b n) -> p b n", b=2) for a in (0, 2048))
                            mask = flat[:, 4096:4160]

                            def fetch(j):
                                pool.dma_start(raw[:, j % 2, :], io["near"][bass.ds(layer * 4 + j, 1)]
                                               .rearrange("a p n -> (a p) n")).then_inc(near_read[j % 2], 16)

                            pool.dma_start(mask, io["column_mask"]).then_inc(mask_in, 16)
                            fetch(0)
                            fetch(1)
                            pool.wait_ge(mask_in, layer * 16 + 16)
                            for j in range(4):
                                pool.wait_ge(near_read[j % 2], layer * 32 + 16 * (j // 2 + 1))
                                if j >= 2:
                                    pool.wait_ge(near_stored[j % 2], layer * 32 + 16)
                                pool.tensor_tensor(out[:, j % 2, :].rearrange("p (v n) -> p v n", n=64),
                                                   mask.rearrange("p (v n) -> p v n", v=1).broadcast_to([128, 14, 64]),
                                                   raw[:, j % 2, :].rearrange("p (v n) -> p v n", n=64), ALU.subtract
                                                   ).then_inc(near_step, 1)
                                pool.wait_ge(near_step, j + 1)
                                pool.dma_start(near_bias[bass.ds(layer * 4 + j, 1)].rearrange("a p n -> (a p) n"),
                                               out[:, j % 2, :]).then_inc(near_stored[j % 2], 16)
                                if j < 2:
                                    fetch(j + 2)

                        pool.memset(ada_part[:, 0:1], 0.0).then_inc(ada_step, 1)
                        neighbourhood_biases()
                        conditioning_half(0)
                        for u, k in comb_of.items():
                            qb, h = u // 16, u % 16
                            if k >= 2:
                                last = [v for v, kk in comb_of.items() if kk == k - 2][0]
                                pool.wait_ge(att.biased, last + 1)
                            if k == 0:
                                pool.wait_ge(small, 64)
                            pool.wait_ge(sel_done, qb)
                            a, e = spans[qb]
                            pool.tensor_tensor(comb[:, k % 2, 0:e - a], far[:, h - 8, 512 - (e - a):512], work[:, a:e],
                                               ALU.add).then_inc(comb_done, 1)
                        pool.wait_ge(att.out_done, 2 * NQ)
                        conditioning_half(1)

                    @block.tensor
                    def _(pe):
                        norms[0].tensor(pe)
                        mlp_a.tensor(pe, lambda eng, s, c: eng.wait_ge(norms[0].lo_done, c + 1))
                        norms[1].tensor(pe)

                        def index_scores():
                            pe.wait_ge(evac, 3)
                            for n, (qb, i) in enumerate((q, i) for q in range(1, NQ) for i in range(4)):
                                nk = 128 * (qb + 1)
                                if n >= 2:
                                    pe.wait_ge(relu_done, n - 1)
                                r = slice(64 * (i % 2), 64 * (i % 2) + 64)
                                pe.matmul(ps[:, 4 + n % 2, 0:nk], QI[r, i // 2, 128 * qb:128 * qb + 128], KI[r, 0:nk],
                                          start=True, stop=True).then_inc(idx_mm, 1)

                        def latent():
                            pe.wait_ge(ckv_sq, 1)
                            pe.matmul(ps[:, 6, :], ones[:, :], relu[:, 0, :], start=True, stop=True).then_inc(ckv_sum, 1)

                        def latent_up():
                            pe.wait_ge(ckv_n, 1)
                            pe.matmul(ps[:, 7, :], upc[:, 0:128], CKV[:, :], start=True, stop=True).then_inc(kv_mm, 1)
                            for j in range(NQ):
                                m = pe.matmul(ps[:, 6, 64 * j:64 * j + 64], CKV[:, 128 * j:128 * j + 128], upc[:, 128:192],
                                              start=True, stop=True)
                            m.then_inc(kv_mm, 1)

                        for j, (kind, dst) in enumerate(order):
                            n = n_mix + j
                            st.ready(pe, n)
                            if j == 0:
                                pe.wait_ge(norms[1].root_done, 1)
                            if j >= 4:
                                pe.wait_ge(evac, j - 3)
                            if kind != "V":
                                for k in range(KC):
                                    if j == 0:
                                        pe.wait_ge(norms[1].lo_done, k + 1)
                                    m = mm3(pe, ps[:, j % 4, :], st.at(n, 128 * k, 128 * k + 128), (Hh[:, k, :], Hl[:, k, :]),
                                            k == 0, k == KC - 1)
                            if kind == "KI":
                                for q in range(NQ):
                                    for k in range(KC):
                                        t = slice(128 * q, 128 * q + 128)
                                        m = mm3(pe, ps[:, 4, 4 * q:4 * q + 4], (Hh[:, k, t], Hl[:, k, t]),
                                                st.at(n, 128 * k + 64, 128 * k + 68), k == 0, k == KC - 1)
                            if kind == "V":
                                for q in range(NQ):
                                    for k in range(KC):
                                        t = slice(128 * q, 128 * q + 128)
                                        m = mm3(pe, ps[:, j % 4, 128 * q:128 * q + 128], (Hh[:, k, t], Hl[:, k, t]),
                                                st.at(n, 128 * k, 128 * k + 128), k == 0, k == KC - 1)
                            m.then_inc(st.used, 1)
                            if j == IDX_AFTER:
                                index_scores()
                            if j == CKV_AFTER + 1:
                                latent()
                            if j == CKV_AFTER + 3:
                                latent_up()

                        def ready(eng):
                            eng.wait_ge(evac, N_IN1)
                            eng.wait_ge(kv_out, 2)
                            eng.wait_ge(relu_done, 12)

                        att.tensor(pe, ready)
                        proj.tensor(pe, lambda eng: (att.all_turned(eng),
                                                     eng.wait_ge(att.out_done, 2 * NQ)))
                        norms[2].tensor(pe)
                        mlp_b.tensor(pe, lambda eng, s, c: eng.wait_ge(norms[2].lo_done, c + 1))

                    @block.scalar
                    def _(act):
                        st.start(st.split_hi, act)
                        norms[0].scalar(act)
                        act.dma_start(upc[:], io["w_kv_up"][bass.ds(layer, 1)].rearrange("a p n -> (a p) n")
                                      ).then_inc(small, 16)
                        head = 128 * 640
                        act.dma_start(near[:], bass.AP(bias_rows.tensor, 383, [[639, 128], [head, 8], [1, 256]])
                                      ).then_inc(small, 16)
                        act.dma_start(far[:], bass.AP(bias_rows.tensor, 8 * head + 127, [[639, 128], [head, 8], [1, 512]])
                                      ).then_inc(small, 16)
                        act.dma_start(tri[:], io["causal"]).then_inc(small, 16)
                        mlp_a.scalar(act)
                        norms[1].scalar(act, mlp_a.x_ready)
                        act.wait_ge(ada_done, 1)
                        for j, (kind, dst) in enumerate(order):
                            n = n_mix + j
                            st.split_hi(act, n + st.n_hl)
                            act.wait_ge(st.used, n + 1)
                            if kind == "V":
                                m = act.activation(dst, ps[:, j % 4, :].rearrange("p (q n) -> p q n", n=128), ACT.Copy)
                            else:
                                for d, a, e, scale in dst:
                                    m = act.activation(d, ps[a:e, j % 4, :], ACT.Copy, scale=scale)
                            if kind == "KI":
                                m = act.activation(WI[:, :, :], ps[:, 4, 0:16].rearrange("p (q n) -> p q n", n=4), ACT.Copy)
                            m.then_inc(evac, 1)
                            if j == IDX_AFTER:
                                for i, (qb, _) in enumerate((q, i) for q in range(1, NQ) for i in range(4)):
                                    nk = 128 * (qb + 1)
                                    act.wait_ge(idx_mm, i + 1)
                                    if i >= 2:
                                        act.wait_ge(acc_done, i - 1)
                                    act.activation(relu[:, i % 2, 0:nk], ps[:, 4 + i % 2, 0:nk], ACT.Relu, scale=1.0 / 16
                                                   ).then_inc(relu_done, 1)
                            if j == CKV_AFTER:
                                act.wait_ge(acc_done, 12)
                                act.wait_ge(evac, 4)
                                act.activation(relu[:, 0, :], CKV[:, :], ACT.Square).then_inc(ckv_sq, 1)
                            if j == CKV_AFTER + 1:
                                act.wait_ge(ckv_sum, 1)
                                act.activation(relu[:, 1, :], ps[:, 6, :], ACT.Ln, bias=eps[:, 0:1], scale=1.0 / 128
                                               ).then_inc(ckv_root, 1)
                                act.wait_ge(ckv_root, 1)
                                act.activation(relu[:, 0, :], relu[:, 1, :], ACT.Exp, scale=-0.5).then_inc(ckv_inv, 1)
                            if j == CKV_AFTER + 3:
                                act.wait_ge(kv_mm, 2)
                                act.activation(KCc[:, :], ps[:, 7, :], ACT.Copy).then_inc(kv_out, 1)
                                act.activation(VC[:, :, :], ps[:, 6, 0:256].rearrange("p (q n) -> p q n", n=64), ACT.Copy
                                               ).then_inc(kv_out, 1)
                        att.scalar(act, lambda eng: eng.wait_ge(evac, N_IN1))
                        proj.scalar(act)
                        norms[2].scalar(act, proj.x_ready)
                        mlp_b.scalar(act)

                    @block.vector
                    def _(dve):
                        def conditioning_sum(half):
                            dve.wait_ge(ada_step, 1 + 6 * 24 * (half + 1))
                            dve.tensor_reduce(mod_flat[:, bass.ds(layer * 96 + 48 * half, 48)],
                                              ada_part.rearrange("p (k n) -> p k n", n=32), AX, ALU.add
                                              ).then_inc(ada_done, 1)

                        st.start(st.split_lo, dve)
                        dve.wait_ge(vecs_in, 16)
                        dve.tensor_scalar(nsink[:, :], lv[:, 25:33], -1.0, None, ALU.mult).then_inc(nsink_done, 1)
                        norms[0].vector(dve)
                        mlp_a.vector(dve)
                        conditioning_sum(0)
                        dve.wait_ge(small, 64)
                        norms[1].vector(dve)
                        rounds = topk_rounds()
                        for j in range(N_IN1):
                            st.split_lo(dve, n_mix + j + st.n_hl)
                            if j == IDX_AFTER:
                                n = 0
                                for qb in range(1, NQ):
                                    a, e = spans[qb]
                                    for i in range(4):
                                        dve.wait_ge(relu_done, n + 1)
                                        w = WI[:, qb, i:i + 1]
                                        if i == 0:
                                            m = dve.tensor_scalar(work[:, a:e], relu[:, n % 2, 0:e - a], w, None, ALU.mult)
                                        else:
                                            dve.wait_ge(acc_done, n)
                                            m = dve.scalar_tensor_tensor(out=work[:, a:e], in0=relu[:, n % 2, 0:e - a],
                                                                         scalar=w, in1=work[:, a:e], op0=ALU.mult,
                                                                         op1=ALU.add)
                                        m.then_inc(acc_done, 1)
                                        n += 1
                                    dve.wait_ge(acc_done, n)
                                    dve.tensor_tensor(work[:, e - 128:e], work[:, e - 128:e], tri[:, :], ALU.add
                                                      ).then_inc(topk, 1)
                            if j > IDX_AFTER:
                                for _ in range(4):
                                    rounds(dve)
                            if j == CKV_AFTER + 1:
                                dve.wait_ge(ckv_inv, 1)
                                dve.scalar_tensor_tensor(out=CKV[:, :], in0=CKV[:, :], scalar=lv[:, 24:25], in1=relu[:, 0, :],
                                                         op0=ALU.mult, op1=ALU.mult).then_inc(ckv_n, 1)
                        while rounds(dve):
                            pass

                        def combined(eng, u):
                            if u == 0:
                                eng.wait_ge(nsink_done, 1)
                            if u in comb_of:
                                eng.wait_ge(comb_done, comb_of[u] + 1)

                        att.vector(dve, combined)
                        proj.vector(dve)
                        norms[2].vector(dve)
                        mlp_b.vector(dve)
                        conditioning_sum(1)

                S.clear()
            S.ctx.close()

        def modulation(layer, half, s):
            return (lambda c: mod_x[:, layer, half, c, s:s + 1]), (lambda c: mod[:, layer, 24 * half + c, s:s + 1])

        def gate(layer, half):
            return lambda s, o: mod[:, layer, 24 * half + 16 + o, s:s + 1]

        def even_layer(CX):
            S = Sems()
            N2 = T + CT
            with ExitStack() as ctx:
                Hh, Hl = sb(ctx, "h_hi", [128, KC, T], F32R), sb(ctx, "h_lo", [128, KC, T], F32R)
                Ch, Cl = sb(ctx, "c_hi", [128, KC, CT], F32R), sb(ctx, "c_lo", [128, KC, CT], F32R)
                QA, KD = sb(ctx, "qa", [128, 4, N2]), sb(ctx, "ka", [128, 2, N2])
                QB, KB = sb(ctx, "qb", [128, 4, N2]), sb(ctx, "kb", [128, 4, N2])
                VA, VB = sb(ctx, "va", [128, 6, 128]), sb(ctx, "vb", [128, 6, 512])
                arena = sb(ctx, "arena", [128, 13 * 512])
                stage = sb(ctx, "near_stage", [128, 2, 512])
                window, zeros = sb(ctx, "window", [128, 384]), sb(ctx, "zeros", [128, 256])
                cos, sin = sb(ctx, "cos", [128, T]), sb(ctx, "sin", [128, T])
                rot = sb(ctx, "rot", [128, 128])
                nsink, gains = sb(ctx, "minus_sinks", [128, 8]), sb(ctx, "gains", [128, 4])
                st = Stream(ctx, S, io["w_even"], 3, 2)
                small, prepared = S("small"), S("prepared")

                def carve(at, shape):
                    n = int(np.prod(shape))
                    v = arena[:, at:at + n]
                    return v if len(shape) == 1 else v.rearrange("p (a n) -> p a n", a=shape[0])

                nt = {"sq": carve(0, [2, T]), "root": carve(2 * T, [T]), "inv": carve(3 * T, [T]),
                      "h": carve(4 * T, [3, T])}
                w = {"raw": carve(0, [2, N2]), "sq": carve(2 * N2, [2, N2]), "root": carve(4 * N2, [N2]),
                     "inv": carve(5 * N2, [N2]), "t": carve(6 * N2, [2, N2]), "cos": carve(8 * N2, [512]),
                     "sin": None}
                w["sin"] = stage[:, 0, :]
                at = attention_temps(ctx, carve(0, [2, N2]), carve(2 * N2, [2, N2]))
                O, q_wide = carve(4 * N2, [2, 512]), carve(4 * N2 + 1024, [4, 128])
                xs = [{"n": T, "h": (Hh, Hl), "x": X}, {"n": CT, "h": (Ch, Cl), "x": CX}]
                norms = []
                for s, stream in enumerate(xs):
                    gain, shift = modulation(0, 0, s)
                    norms.append(Norm(S, nt, lambda c, x=stream["x"]: x[:, c, :], stream["n"], gain, shift,
                                      lambda part, c, h=stream["h"]: h[part][:, c, :], bank=7))

                def feature_tile(pe, i, done):
                    st.ready(pe, i)
                    b = 2 * (i % 2)
                    for s, stream in enumerate(xs):
                        for k in range(KC):
                            if i == 0:
                                pe.wait_ge(norms[s].lo_done, k + 1)
                            hh, hl = stream["h"]
                            m = mm3(pe, ps[:, b + s, 0:stream["n"]], st.at(i, 128 * k, 128 * k + 128),
                                    (hh[:, k, :], hl[:, k, :]), k == 0, k == KC - 1)
                    m.then_inc(done, 1)

                def token_tile(pe, i, done):
                    st.ready(pe, i)
                    for j in range(6):
                        hh, hl = xs[j // 4]["h"]
                        t = slice(128 * (j % 4), 128 * (j % 4) + 128)
                        for k in range(KC):
                            m = mm3(pe, ps[:, 2 * (i % 2) + j // 4, 128 * (j % 4):128 * (j % 4) + 128],
                                    (hh[:, k, t], hl[:, k, t]), st.at(i, 128 * k, 128 * k + 128), k == 0, k == KC - 1)
                    m.then_inc(done, 1)

                def token_pair(pe, i, done):
                    n = items[i]["tiles"][0]
                    st.ready(pe, n + 1)
                    pe.wait_ge(heads.raw_done, i)
                    for j in range(6):
                        hh, hl = xs[j // 4]["h"]
                        t = slice(128 * (j % 4), 128 * (j % 4) + 128)
                        bank = 2 * (i % 2) + j // 2 if j < 4 else 7
                        out = ps[:, bank, 256 * (j % 2):256 * (j % 2) + 256].rearrange("p (a n) -> p a n", a=2)
                        for k in range(KC):
                            m = mm3(pe, out, (hh[:, k, t], hl[:, k, t]), st.pair_at(128 * k, 128 * k + 128),
                                    k == 0, k == KC - 1)
                    m.then_inc(done, 2)

                every = slice(0, 128)

                def head_item(i, dst, gain, rope):
                    return {"project": feature_tile, "n": N2, "plain": False, "ones": head_ones[:, :],
                            "scale": 1.0 / HD, "gain": gain, "rope": rope, "dst": dst, "tiles": [i]}

                def value_item(i, dst):
                    return {"project": token_tile, "n": N2, "plain": True, "rope": False, "tiles": [i],
                            "copies": lambda k: [(dst, ps[:, 2 * (k % 2):2 * (k % 2) + 2, :]
                                                  .rearrange("p a n -> p (a n)")[:, 0:N2]
                                                  .rearrange("p (q n) -> p q n", n=128), 1.0)]}

                items = []
                for c in range(4):
                    items.append(head_item(c, [(every, lambda a, b, c=c: QA[:, c, a:b])], gains[:, 0:1], True))
                items.append(head_item(4, [(slice(64 * g, 64 * g + 64), lambda a, b, g=g, d=d: KD[64 * d:64 * d + 64, g, a:b])
                                           for g in range(2) for d in range(2)], gains[:, 1:2], True))
                items.append(value_item(5, VA[:, :, :]))
                for c in range(4):
                    items.append(head_item(6 + c, [(every, lambda a, b, c=c: QB[:, c, a:b])], gains[:, 2:3], False))
                for c in range(4):
                    items.append(head_item(10 + c, [(every, lambda a, b, c=c: KB[:, c, a:b])], gains[:, 3:4], False))
                for c in range(2):
                    def copies(k, c=c):
                        v = VB[:, :, 256 * c:256 * c + 256]
                        own = ps[:, 2 * (k % 2):2 * (k % 2) + 2, :].rearrange("p a n -> p (a n)")
                        return [(v[:, 0:4, :], own.rearrange("p (q n) -> p q n", n=256), 1.0),
                                (v[:, 4:6, :], ps[:, 7, :].rearrange("p (q n) -> p q n", n=256), 1.0)]
                    items.append({"project": token_pair, "n": N2, "plain": True, "rope": False,
                                  "tiles": [14 + 2 * c, 15 + 2 * c], "copies": copies})
                heads = HeadTiles(S, w, st, items, rot[:, :], cos[:, :], sin[:, :])

                units, staged = [], {}
                for qb in range(NQ):
                    for h in range(16):
                        r = slice(64 * (h % 2), 64 * (h % 2) + 64)
                        qs = slice(128 * qb, 128 * qb + 128)
                        if h < 8:
                            a, e = max(0, qb - 1), min(NQ, qb + 2)
                            u0 = 128 * (a - qb + 1)
                            n = 128 * (e - a)
                            v = slice(64 * (h // 4), 64 * (h // 4) + 64)
                            units.append({"q": QA[r, h // 2, qs], "init": nsink[:, h:h + 1],
                                          "keys": [(KD[:, h // 4, 128 * a:128 * e], 0, n, window[:, u0:u0 + n]),
                                                   (KD[:, h // 4, T:N2], 512, CT, zeros[:, :])],
                                          "v": [VA[:, j, v] for j in [*range(a, e), 4, 5]]})
                        else:
                            k = len(staged)
                            staged[len(units)] = (k, h - 8, qb)
                            v = slice(64 * (h - 8), 64 * (h - 8) + 64)
                            units.append({"q": QB[r, (h - 8) // 2, qs], "init": NO_MAX,
                                          "keys": [(KB[:, (h - 8) // 2, 0:T], 0, T, stage[:, k % 2, :]),
                                                   (KB[:, (h - 8) // 2, T:N2], 512, CT, zeros[:, :])],
                                          "v": [VB[:, j, v] for j in range(6)]})
                for cb in range(CT // 128):
                    for h in range(16):
                        r = slice(64 * (h % 2), 64 * (h % 2) + 64)
                        qs = slice(T + 128 * cb, T + 128 * cb + 128)
                        q, k = (QA[r, h // 2, qs], KD[:, h // 4, T:N2]) if h < 8 else \
                            (QB[r, (h - 8) // 2, qs], KB[:, (h - 8) // 2, T:N2])
                        v = [VA[:, j, 64 * (h // 4):64 * (h // 4) + 64] if h < 8 else
                             VB[:, j, 64 * (h - 8):64 * (h - 8) + 64] for j in (4, 5)]
                        units.append({"q": q, "init": nsink[:, h:h + 1] if h < 8 else NO_MAX,
                                      "keys": [(k, 0, CT, zeros[:, :])], "v": v})
                n_groups = len(units) // 8
                groups = [{"out": O[:, g % 2, :].rearrange("p (a b d) -> p a b d", a=1, d=64), "shape": (1, 8),
                           "minus_sinks": nsink[:, :] if g % 2 == 0 else None,
                           "free_after": 2 * (g // 2) if g >= 2 else None} for g in range(n_groups)]
                turns = {}
                for b in range(n_groups // 2):
                    hh, hl = xs[b // 4]["h"]
                    t = slice(128 * (b % 4), 128 * (b % 4) + 128)
                    turns[2 * b + 1] = [(O[:, c // 4, 128 * (c % 4):128 * (c % 4) + 128], hh[:, c, t], hl[:, c, t])
                                        for c in range(8)]
                att = Attention(S, at, units, groups, turns, q_wide)
                proj = Project(S, st, N_INE, xs, gate(0, 0))
                near_in = near_staged

                with nc.Block() as block:
                    @block.sync
                    def _(sp):
                        for dst, src in ((window, "window"), (cos, "cos"), (sin, "sin"), (rot, "rotation")):
                            sp.dma_start(dst[:], io[src]).then_inc(small, 16)
                        st.load(sp)

                    @block.gpsimd
                    def _(pool):
                        heads.all_out(pool)
                        for u, (k, h, qb) in staged.items():
                            if k >= 2:
                                last = [v for v, x in staged.items() if x[0] == k - 2][0]
                                pool.wait_ge(att.biased, last + 1)
                            a = 64 * (6 - 2 * qb)
                            pool.dma_start(stage[:, k % 2, :], near_bias[h][:, a:a + 512]).then_inc(near_in[k % 2], 16)

                    @block.tensor
                    def _(pe):
                        norms[0].tensor(pe)
                        pe.wait_ge(norms[0].root_done, 1)
                        norms[1].tensor(pe)
                        pe.wait_ge(small, 64)
                        heads.tensor(pe)
                        att.tensor(pe, heads.all_out)
                        proj.tensor(pe, lambda eng: (att.all_turned(eng), eng.wait_ge(att.out_done, n_groups)))

                    @block.scalar
                    def _(act):
                        st.start(st.split_hi, act)
                        norms[0].scalar(act)
                        norms[1].scalar(act)
                        heads.scalar(act)
                        att.scalar(act, heads.all_out)
                        proj.scalar(act)

                    @block.vector
                    def _(dve):
                        st.start(st.split_lo, dve)
                        dve.memset(zeros[:, :], 0.0).then_inc(prepared, 1)
                        dve.tensor_scalar(nsink[:, :], vec("a_sink", 8), -1.0, None, ALU.mult).then_inc(prepared, 1)
                        for j, (key, scale) in enumerate((("a_q_norm", -0.125), ("a_k_norm", 1.0),
                                                          ("b_q_norm", -0.125), ("b_k_norm", 1.0))):
                            dve.tensor_scalar(gains[:, j:j + 1], vec(key, 1), scale, None, ALU.mult).then_inc(prepared, 1)
                        dve.wait_ge(prepared, 6)
                        norms[0].vector(dve)
                        norms[1].vector(dve)
                        dve.wait_ge(small, 64)
                        heads.vector(dve)

                        def staged_bias(eng, u):
                            if u in staged:
                                k = staged[u][0]
                                eng.wait_ge(near_in[k % 2], 16 * (k // 2 + 1))
                        att.vector(dve, staged_bias, heads.all_out)
                        proj.vector(dve)
                S.close()

        def mlp_layer(layer, CX):
            S = Sems()
            with ExitStack() as ctx:
                xs = [{"n": T, "x": X}] + ([{"n": CT, "x": CX}] if layer < DEPTH - 1 else [])
                for stream in xs:
                    stream["h"] = (sb(ctx, "h_hi", [128, KC, stream["n"]], F32R),
                                   sb(ctx, "h_lo", [128, KC, stream["n"]], F32R))
                st = Stream(ctx, S, io["w_mlp"], 4, 4, MLP_TILES)
                scratch = sb(ctx, "scratch", [128, 7, T])
                nt = {"sq": scratch[:, 0:2, :], "root": scratch[:, 2, :], "inv": scratch[:, 3, :],
                      "h": scratch[:, 4:7, :]}
                norms = []
                for s, stream in enumerate(xs):
                    gain, shift = modulation(layer, 1, s)
                    norms.append(Norm(S, nt, lambda c, x=stream["x"]: x[:, c, :], stream["n"], gain, shift,
                                      lambda part, c, h=stream["h"]: h[part][:, c, :], bank=7))
                mlp = Mlp(ctx, S, st, 0, xs, False, gate(layer, 1))
                with nc.Block(no_gpsimd_drain=True) as block:
                    @block.sync
                    def _(sp):
                        st.load(sp, layer * MLP_TILES)

                    @block.tensor
                    def _(pe):
                        for s, norm in enumerate(norms):
                            if s:
                                pe.wait_ge(norms[s - 1].root_done, 1)
                            norm.tensor(pe)
                        mlp.tensor(pe, lambda eng, s, c: eng.wait_ge(norms[s].lo_done, c + 1))

                    @block.scalar
                    def _(act):
                        st.start(st.split_hi, act)
                        for norm in norms:
                            norm.scalar(act)
                        mlp.scalar(act)

                    @block.vector
                    def _(dve):
                        st.start(st.split_lo, dve)
                        for norm in norms:
                            norm.vector(dve)
                        mlp.vector(dve)
                S.close()

        def odd_layer(CX):
            S = Sems()
            N2 = T + CT
            with ExitStack() as ctx:
                Hh, Hl = sb(ctx, "h_hi", [128, KC, T], F32R), sb(ctx, "h_lo", [128, KC, T], F32R)
                Ch, Cl = sb(ctx, "c_hi", [128, KC, CT], F32R), sb(ctx, "c_lo", [128, KC, CT], F32R)
                Qh, Ql = sb(ctx, "cq_hi", [128, 3, T], F32R), sb(ctx, "cq_lo", [128, 3, T], F32R)
                Lh, Ll = sb(ctx, "ckv_hi", [128, 2, N2], F32R), sb(ctx, "ckv_lo", [128, 2, N2], F32R)
                Q, K = sb(ctx, "q", [128, 8, T]), sb(ctx, "k", [128, 8, N2])
                V = sb(ctx, "v", [128, 6, 512])
                arena = sb(ctx, "arena", [128, 6 * N2 + 512])
                cos, sin = sb(ctx, "cos", [128, T]), sb(ctx, "sin", [128, T])
                rot, mla_ones = sb(ctx, "rot", [128, 128]), sb(ctx, "mla_ones", [128, 128])
                zeros = sb(ctx, "zeros", [128, 512])
                gq = sb(ctx, "q_gain", [128, 1])
                st = Stream(ctx, S, io["w_odd"], 3, 2)
                small, prepared = S("small"), S("prepared")

                def carve(at, shape):
                    n = int(np.prod(shape))
                    v = arena[:, at:at + n]
                    return v if len(shape) == 1 else v.rearrange("p (a n) -> p a n", a=shape[0])

                cx = CX[:, :, :].rearrange("p a n -> p (a n)")
                nt = {"sq": carve(0, [2, T]), "root": carve(2 * T, [T]), "inv": carve(3 * T, [T]),
                      "h": carve(4 * T, [3, T])}
                w = {"raw": cx[:, 0:2 * N2].rearrange("p (a n) -> p a n", a=2), "sin": cx[:, 2 * N2:2 * N2 + 512],
                     "sq": carve(0, [2, N2]), "root": carve(2 * N2, [N2]), "inv": carve(3 * N2, [N2]),
                     "t": carve(4 * N2, [2, N2]), "cos": carve(6 * N2, [512])}
                at = attention_temps(ctx, carve(0, [2, N2]), carve(2 * N2, [2, N2]))
                O = carve(4 * N2, [2, 512])
                xs = [{"n": T, "h": (Hh, Hl), "x": X}, {"n": CT, "h": (Ch, Cl), "x": CX}]
                norms = []
                for s, stream in enumerate(xs):
                    gain, shift = modulation(1, 0, s)
                    norms.append(Norm(S, nt, lambda c, x=stream["x"]: x[:, c, :], stream["n"], gain, shift,
                                      lambda part, c, h=stream["h"]: h[part][:, c, :], bank=7))
                raw_q = [V[:, :, :].rearrange("p a n -> p (a n)")[:, 512 * c:512 * c + 512] for c in range(3)]
                raw_k = [V[:, :, :].rearrange("p a n -> p (a n)")[:, 1536 + N2 * c:1536 + N2 * c + N2] for c in range(2)]
                norms.append(Norm(S, nt, lambda c: raw_q[c], T, lambda c: vec("qa_norm", 1, c), None,
                                  lambda part, c: (Qh, Ql)[part][:, c, :], bank=6, nk=3))
                norms.append(Norm(S, nt, lambda c: raw_k[c][:, 0:T], T, lambda c: vec("kva_norm", 1, c), None,
                                  lambda part, c: (Lh, Ll)[part][:, c, 0:T], bank=7, nk=2))
                norms.append(Norm(S, nt, lambda c: raw_k[c][:, T:N2], CT, lambda c: vec("kva_norm", 1, c), None,
                                  lambda part, c: (Lh, Ll)[part][:, c, T:N2], bank=5, nk=2))
                latents = [(raw_q[0], 1), (raw_q[1], 1), (raw_q[2], 1), (raw_k[0], 2), (raw_k[1], 2)]
                lat_done = S("latents")

                def project_x(pe, i, bank, streams):
                    st.ready(pe, i)
                    for s, stream in enumerate(streams):
                        for k in range(KC):
                            if i == 0 or (i == 3 and s == 1):
                                pe.wait_ge(norms[s].lo_done, k + 1)
                            hh, hl = stream["h"]
                            m = mm3(pe, ps[:, bank + s, 0:stream["n"]], st.at(i, 128 * k, 128 * k + 128),
                                    (hh[:, k, :], hl[:, k, :]), k == 0, k == KC - 1)
                    return m

                def kr_tile(pe, i, done):
                    project_x(pe, 5, 2 * (i % 2), xs).then_inc(done, 1)

                def q_tile(n, h):
                    def go(pe, i, done):
                        st.ready(pe, n)
                        for k in range(3):
                            m = mm3(pe, ps[:, 2 * (i % 2), :], st.at(n, 256 * k + 128 * h, 256 * k + 128 * h + 128),
                                    (Qh[:, k, :], Ql[:, k, :]), k == 0, k == 2)
                        m.then_inc(done, 1)
                    return go

                def k_tile(n):
                    def go(pe, i, done):
                        st.ready(pe, n)
                        for s, (a, e) in enumerate(((0, T), (T, N2))):
                            for k in range(2):
                                m = mm3(pe, ps[:, 2 * (i % 2) + s, 0:e - a], st.at(n, 256 * k, 256 * k + 128),
                                        (Lh[:, k, a:e], Ll[:, k, a:e]), k == 0, k == 1)
                        m.then_inc(done, 1)
                    return go

                def v_tile(n):
                    def go(pe, i, done):
                        for j in range(6):
                            t = slice(128 * j, 128 * j + 128)
                            for k in range(2):
                                m = mm3(pe, ps[:, 2 * (i % 2) + j // 4, 128 * (j % 4):128 * (j % 4) + 128],
                                        (Lh[:, k, t], Ll[:, k, t]), st.at(n, 256 * k + 128, 256 * k + 256), k == 0, k == 1)
                        m.then_inc(done, 1)
                    return go

                kr_rows = slice(64, 96)
                heads, atts = [], []
                for half in range(2):
                    items = []
                    if half == 0:
                        items.append({"project": kr_tile, "n": N2, "plain": False, "ones": mla_ones[:, :], "scale": 1.0,
                                      "gain": vec("kr_norm", 1), "rope": True, "tiles": [5],
                                      "dst": [(kr_rows, lambda a, b, h=h: K[64:96, h, a:b]) for h in range(8)]})
                    for p in range(4):
                        n = 6 + 2 * (4 * half + p)
                        for h in range(2):
                            items.append({"project": q_tile(n, h), "n": T, "plain": False, "ones": mla_ones[:, :],
                                          "scale": 1.0, "gain": gq[:, 0:1], "rope": True, "tiles": [] if h == 0 else [n],
                                          "dst": [(slice(0, 96), lambda a, b, c=2 * p + h: Q[0:96, c, a:b])]})
                        items.append({"project": k_tile(n + 1), "n": N2, "plain": False, "ones": head_ones[:, :],
                                      "scale": 1.0 / HD, "gain": vec("kn_norm", 1), "rope": False, "tiles": [],
                                      "dst": [(slice(64 * h, 64 * h + 64), lambda a, b, c=2 * p + h: K[0:64, c, a:b])
                                              for h in range(2)]})
                        items.append({"project": v_tile(n + 1), "n": N2, "plain": True, "rope": False, "tiles": [n + 1],
                                      "copies": lambda k, p=p: [(V[:, :, 128 * p:128 * p + 128],
                                                                 ps[:, 2 * (k % 2):2 * (k % 2) + 2, :]
                                                                 .rearrange("p a n -> p (a n)")[:, 0:N2]
                                                                 .rearrange("p (q n) -> p q n", n=128), 1.0)]})
                    heads.append(HeadTiles(S, w, st, items, rot[:, :], cos[:, :], sin[:, :]))
                    units = [{"q": Q[:, h, 128 * qb:128 * qb + 128], "init": NO_MAX,
                              "keys": [(K[:, h, 0:T], 0, T, zeros[:, :]), (K[:, h, T:N2], 512, CT, zeros[:, 0:CT])],
                              "v": [V[:, j, 64 * h:64 * h + 64] for j in range(6)]}
                             for qb in range(NQ) for h in range(8)]
                    groups = [{"out": O[:, g % 2, :].rearrange("p (a b d) -> p a b d", a=1, d=64), "shape": (1, 8),
                               "minus_sinks": None, "free_after": g - 1 if g >= 2 else None} for g in range(NQ)]
                    turns = {g: [(O[:, g % 2, 128 * c:128 * c + 128],
                                  Hh[:, 4 * half + c, 128 * g:128 * g + 128], Hl[:, 4 * half + c, 128 * g:128 * g + 128])
                                 for c in range(4)] for g in range(NQ)}
                    atts.append(Attention(S, at, units, groups, turns))
                proj = Project(S, st, 6 + 2 * ODD_PAIRS, xs[:1], gate(1, 0))

                with nc.Block(no_gpsimd_drain=True) as block:
                    @block.sync
                    def _(sp):
                        for dst, src in ((cos, "mla_cos"), (sin, "mla_sin"), (rot, "mla_rotation"),
                                         (mla_ones, "mla_ones")):
                            sp.dma_start(dst[:], io[src]).then_inc(small, 16)
                        st.load(sp)

                    @block.tensor
                    def _(pe):
                        norms[0].tensor(pe)
                        pe.wait_ge(norms[0].root_done, 1)
                        norms[1].tensor(pe)
                        for i, (_, ns) in enumerate(latents):
                            if i >= 2:
                                pe.wait_ge(lat_done, i - 1)
                            project_x(pe, i, 2 * (i % 2), xs[:ns]).then_inc(st.used, 1)
                        for norm in norms[2:]:
                            norm.tensor(pe)
                        pe.wait_ge(small, 64)
                        for half in range(2):
                            if half == 0:
                                for norm in norms[2:]:
                                    pe.wait_ge(norm.lo_done, norm.nk)
                            else:
                                pe.wait_ge(atts[0].exped, 32)
                                pe.wait_ge(atts[0].chunk_lo, atts[0].turn_total)
                                pe.wait_ge(atts[0].out_done, NQ)
                            heads[half].tensor(pe)
                            atts[half].tensor(pe, heads[half].all_out)
                        proj.tensor(pe, lambda eng: (atts[1].all_turned(eng), eng.wait_ge(atts[1].out_done, NQ)))

                    @block.scalar
                    def _(act):
                        st.start(st.split_hi, act)
                        norms[0].scalar(act)
                        norms[1].scalar(act)
                        for i, (dst, ns) in enumerate(latents):
                            st.split_hi(act, i + st.n_hl)
                            act.wait_ge(st.used, i + 1)
                            act.activation(dst, ps[:, 2 * (i % 2):2 * (i % 2) + 2, :].rearrange("p a n -> p (a n)")
                                           [:, 0:T if ns == 1 else N2], ACT.Copy).then_inc(lat_done, 1)
                        for k, norm in enumerate(norms[2:]):
                            norm.scalar(act, lambda eng, c: eng.wait_ge(lat_done, 5))
                        for half in range(2):
                            heads[half].scalar(act)
                            atts[half].scalar(act)
                        proj.scalar(act)

                    @block.vector
                    def _(dve):
                        st.start(st.split_lo, dve)
                        dve.memset(zeros[:, :], 0.0).then_inc(prepared, 1)
                        dve.memset(Q[96:128, :, :], 0.0).then_inc(prepared, 1)
                        dve.memset(K[96:128, :, :], 0.0).then_inc(prepared, 1)
                        dve.tensor_scalar(gq[:, :], vec("q_norm", 1), -(96 ** -0.5), None, ALU.mult
                                          ).then_inc(prepared, 1)
                        dve.wait_ge(prepared, 4)
                        norms[0].vector(dve)
                        norms[1].vector(dve)
                        for i in range(5):
                            st.split_lo(dve, i + st.n_hl)
                        for norm in norms[2:]:
                            norm.vector(dve)
                        dve.wait_ge(small, 64)
                        for half in range(2):
                            heads[half].vector(dve)
                            atts[half].vector(dve)
                        proj.vector(dve)
                S.close()

        def store():
            S = Sems()
            with nc.Block(no_gpsimd_drain=True) as block:
                stored = S("stored")

                @block.sync
                def _(sp):
                    sp.dma_start(io["out"], X[:]).then_inc(stored, 16)
                    sp.wait_ge(stored, 16)
            S.close()

        setup()
        first_block()
        with ExitStack() as second:
            CX = sb(second, "ctx_x", [128, KC, CT])
            conditioning(CX)
            even_layer(CX)
            mlp_layer(0, CX)
            odd_layer(CX)
            mlp_layer(1, CX)
            store()


def _bucket(dist):
    f = np.float32
    n = np.maximum(dist, 0)
    large = 16 + (np.log(np.maximum(n, 1).astype(f) / f(16)) / f(np.log(8.0)) * f(16)).astype(np.int32)
    return np.where(n < 16, n, np.minimum(large, 31))


def _rope(width, rows_of_heads, first):
    half = width // 4
    cos, sin = np.ones((128, T), np.float32), np.zeros((128, T), np.float32)
    rot = np.zeros((128, 128), np.float32)
    inv = np.float32(10000.0) ** (-np.arange(half, dtype=np.float32) / np.float32(half))
    t = np.arange(T)
    for base in rows_of_heads:
        for part, pos in ((0, t // 64), (1, t % 64)):
            a = first + base + part * 2 * half
            ang = pos.astype(np.float32)[None, :] * inv[:, None]
            for s in range(2):
                cos[a + s * half:a + (s + 1) * half] = np.cos(ang)
                sin[a + s * half:a + (s + 1) * half] = np.sin(ang)
            for d in range(half):
                rot[a + half + d, a + d] = -1.0
                rot[a + d, a + half + d] = 1.0
    return cos, sin, rot


def _constants():
    f = np.float32
    c = {"ident": np.eye(128, dtype=f), "ones": np.ones((128, 128), f)}
    c["head_ones"] = np.kron(np.eye(2, dtype=f), np.ones((64, 64), f))
    m = np.zeros((128, 128), f)
    m[0:64, 0:64] = 1 / 64
    m[64:96, 64:96] = 1 / 32
    c["mla_ones"] = m
    dist = 511 - np.arange(640)
    lines = np.zeros((33, 2, 640), f)
    for a, ok in enumerate(((dist >= 0) & (dist < 128), dist >= 0)):
        lines[_bucket(dist)[ok], a, np.nonzero(ok)[0]] = -1.0
        lines[32, a, ~ok] = BIG
    c["bucket_lines"] = lines
    q, k = np.arange(128)[:, None], np.arange(128)[None, :]
    c["causal"] = np.where(k <= q, 0, -BIG).astype(f)
    cq = (np.arange(128) % 64)[:, None]
    c0 = np.clip(cq - 8, 0, 48)
    ck = np.arange(64)[None, :]
    c["column_mask"] = np.where((ck >= c0) & (ck < c0 + 16), 0, BIG).astype(f)
    u = np.arange(384)[None, :]
    c["window"] = np.where(np.abs(128 + q - u) <= 128, 0, BIG).astype(f)
    c["cos"], c["sin"], c["rotation"] = _rope(64, (0, 64), 0)
    c["mla_cos"], c["mla_sin"], c["mla_rotation"] = _rope(32, (0,), 64)
    return c


def _cols(v):
    return np.ascontiguousarray(v.reshape(-1, 128).T)


def _k_tiles(w):
    return w.reshape(8, 128, -1, 128).transpose(2, 1, 0, 3).reshape(-1, 128, 1024)


def _pair_tiles(w):
    return w.reshape(-1, 2, 128, 2, 512).transpose(0, 3, 2, 1, 4).reshape(-1, 2, 128, 1024)


def _interleave(ups, down):
    out = [ups[0]]
    for c in range(1, len(ups)):
        out += [ups[c], down[c - 1]]
    return np.concatenate(out + [down[-1]])


def _swiglu_tiles(gate, up, down):
    g, u = _k_tiles(gate), _k_tiles(up)
    return _interleave([np.stack([g[2 * c], u[2 * c], g[2 * c + 1], u[2 * c + 1]]) for c in range(CH1)],
                       _pair_tiles(down))


def _mlp_tiles(w1, w2):
    a = _k_tiles(w1)
    return _interleave([a[2 * c:2 * c + 2] for c in range(CH2)], _pair_tiles(w2))


def _out_tiles(w):
    return _pair_tiles(w).transpose(1, 0, 2, 3).reshape(-1, 128, 1024)


def _pad_cols(w, n):
    out = np.zeros(w.shape[:-1] + (n,), w.dtype)
    out[..., :w.shape[-1]] = w
    return out


def _lay_out(i):
    f = np.float32
    t = {}
    feat = lambda x: np.ascontiguousarray(x.T.reshape(8, 128, -1).transpose(1, 0, 2))
    t["x"], t["ctx"] = feat(i["x"][0]), feat(i["ctx_2"][0])
    first = []
    order = [15, 16, 17, 14, 4, 5, 0, 1, 2, 3, 6, 7, 8, 9, 10, 11, 12, 13]
    for l in range(DEPTH):
        first += [_swiglu_tiles(i["ffn1_w_gate"][l], i["ffn1_w_up"][l], i["ffn1_w_down"][l]),
                  _k_tiles(_pad_cols(i["w_in"][l], N_IN1 * 128))[order], _out_tiles(i["w_out"][l]),
                  _swiglu_tiles(i["ffn2_w_gate"][l], i["ffn2_w_up"][l], i["ffn2_w_down"][l])]
    t["w_first"] = np.concatenate(first)
    t["w_ada"] = np.concatenate([i["ada_w_2"][l].T.reshape(48, 128, 1024) for l in range(DEPTH)])
    t["w_even"] = np.concatenate([_k_tiles(i["e_w_in_2"][0]), _out_tiles(i["e_w_out_2"][0])])
    t["w_mlp"] = np.concatenate([_mlp_tiles(i["mlp_w1_2"][l], i["mlp_w2_2"][l]) for l in range(DEPTH)])
    w = i["o_w_in_2"][0]
    kr = np.zeros((1024, 128), f)
    kr[:, 64:96] = w[:, 640:672]
    odd = [_k_tiles(np.concatenate([w[:, :640], kr], 1))]
    uq = _pad_cols(i["o_w_uq_2"][0].reshape(3, 128, 16, 96), 128)
    ukv = i["o_w_ukv_2"][0].reshape(2, 128, 16, 2, 64)
    for p in range(ODD_PAIRS):
        q = uq[:, :, 2 * p:2 * p + 2].transpose(1, 0, 2, 3).reshape(128, 768)
        kv = ukv[:, :, 2 * p:2 * p + 2].transpose(1, 0, 3, 2, 4).reshape(128, 512)
        odd.append(np.stack([_pad_cols(q, 1024), _pad_cols(kv, 1024)]))
    t["w_odd"] = np.concatenate(odd + [_out_tiles(i["o_w_out_2"][0])])
    every = lambda v: np.broadcast_to(v, (128, v.shape[-1]))
    t["layer_vecs"] = np.stack([np.concatenate(
        [_cols(i["ffn1_norm"][l]), _cols(i["mix_norm"][l]), _cols(i["ffn2_norm"][l]), _cols(i["kv_norm_c"][l]),
         every(i["attn_sinks"][l])], 1) for l in range(DEPTH)])
    t["w_kv_up"] = np.concatenate([i["w_kv_up_c"][:, :, :64], i["w_kv_up_c"][:, :, :64], i["w_kv_up_c"][:, :, 64:]], 2)
    t["bias_table"] = np.concatenate([i["rel_bias_table"], np.ones((1, 16), f)], 0)
    rpb = i["b_rpb_2"][0]
    lines = np.zeros((8, 15, 128), f)
    lines[:, :, 48:79] = rpb
    a, cq, v, ck = np.ix_(np.arange(2), np.arange(64), np.arange(14), np.arange(64))
    t["near"] = lines.reshape(8, 1920)[:, (1 - a + v) * 128 + 63 - cq + ck].reshape(8, 128, 896)
    zero = lambda n: np.zeros(n, f)
    cat = lambda *a: np.concatenate(a)
    t["cond"] = np.stack([i["c_2"][0], i["c_ctx_2"]])
    qn, qr = i["o_qn_nope_2"][0], i["o_qn_rope_2"][0]
    kn, kr = i["o_kn_nope_2"][0], i["o_kn_rope_2"][0]
    vecs = {"final_norm": _cols(i["final_norm"]), "a_sink": every(i["a_sink_2"][0]),
            "a_q_norm": _cols(cat(i["a_q_norm_2"][0], i["a_q_norm_2"][0])),
            "a_k_norm": _cols(cat(i["a_k_norm_2"][0], i["a_k_norm_2"][0])),
            "b_q_norm": _cols(cat(i["b_q_norm_2"][0], i["b_q_norm_2"][0])),
            "b_k_norm": _cols(cat(i["b_k_norm_2"][0], i["b_k_norm_2"][0])),
            "qa_norm": _cols(i["o_qa_norm_2"][0]), "kva_norm": _cols(i["o_kva_norm_2"][0]),
            "q_norm": _cols(cat(qn, qr, zero(32))), "kr_norm": _cols(cat(zero(64), kr, zero(32))),
            "kn_norm": _cols(cat(kn, kn))}
    for l in range(DEPTH):
        vecs[f"ada_b{l}"] = _cols(i["ada_b_2"][l])
        vecs[f"norm_mix{l}"], vecs[f"norm_mlp{l}"] = _cols(i["norm_mix_2"][l]), _cols(i["norm_mlp_2"][l])
    at, where = 0, {}
    for k, v in vecs.items():
        where[k] = at
        at += v.shape[1]
    t["vecs"] = np.concatenate(list(vecs.values()), 1)
    t.update(_constants())
    return t, where


def kernel(**inputs):
    import concourse.bacc as bacc
    from concourse.bass_utils import run_bass_kernel_spmd

    tensors, where = _lay_out({k: np.asarray(v) for k, v in inputs.items()})
    nc = bacc.Bacc("TRN2", target_bir_lowering=False, num_devices=1)
    io, arrays = {"vec_at": where}, {}
    for k, v in tensors.items():
        arrays[f"in_{k}"] = np.ascontiguousarray(v)
        io[k] = nc.dram_tensor(f"in_{k}", v.shape, F32, kind="ExternalInput").ap()
    io["out"] = nc.dram_tensor("out", (128, KC, T), F32, kind="ExternalOutput").ap()
    program(nc, io)
    r = run_bass_kernel_spmd(nc, [arrays], core_ids=[0])
    out = r.results[0]["out"]
    return np.ascontiguousarray(out.transpose(2, 1, 0).reshape(1, T, D))
```
